# Optimizing a Trainium2 kernel written in Bass

```python
import math
import jax
import jax.numpy as jnp
from jax import lax
import numpy as np

D_MODEL = 2048
BATCH = 1
SEQ = 256
DEPTH = 2

HEAD_DIM = 128
N_SLOTS = D_MODEL // HEAD_DIM
N_EVEN = (DEPTH + 1) // 2
N_ODD = DEPTH // 2
NSA_HEADS = 8
NSA_GROUPS = 2
NSA_HPG = NSA_HEADS // NSA_GROUPS
CMP_BLOCK = 32
CMP_STRIDE = 16
CMP_HIDDEN = 256
SEL_BLOCK = 64
SEL_TOP_N = 16
WINDOW = 512
MLA_HEADS = 8
MLA_Q_RANK = 512
MLA_KV_RANK = 256
MLA_NOPE = 128
MLA_ROPE = 64
MLA_V = 128
DSA_HEADS = 16
DSA_KV_HEADS = 4
IDX_HEADS = 16
IDX_DIM = 64
IDX_ROPE = 32
DSA_TOPK_MAX = 256
REL_BUCKETS = 32
REL_MAX_DIST = 128
FFN_HIDDEN = 4096
CONV_WIDTH = 3
ROPE_THETA = 10000.0
EPS = 1e-6
Q_BLOCK = 128
NEG = -1e30
FORCE = 1e9

EVEN_COLS = NSA_HEADS * HEAD_DIM + 6 * NSA_GROUPS * HEAD_DIM + 3 * NSA_HEADS + MLA_Q_RANK + MLA_KV_RANK + MLA_ROPE
EVEN_OUT = NSA_HEADS * HEAD_DIM + MLA_HEADS * MLA_V
ODD_COLS = DSA_HEADS * HEAD_DIM + 2 * DSA_KV_HEADS * HEAD_DIM + IDX_HEADS * IDX_DIM + IDX_DIM + IDX_HEADS
ODD_OUT = DSA_HEADS * HEAD_DIM

kernel_name = "hybrid_nsa_mla_dsa_convffn"

def _offsets(sizes):
    return [int(v) for v in np.cumsum(sizes)[:-1]]

def rms_norm(x, g):
    xf = x.astype(jnp.float32)
    y = xf * lax.rsqrt(jnp.mean(xf * xf, axis=-1, keepdims=True) + EPS)
    return (y * g.astype(jnp.float32)).astype(x.dtype)

def masked_softmax(logits, mask):
    lf = jnp.where(mask, logits.astype(jnp.float32), NEG)
    p = jax.nn.softmax(lf, axis=-1)
    return p * jnp.any(mask, axis=-1, keepdims=True)

def t5_bucket(dist):
    n = jnp.maximum(dist, 0)
    max_exact = REL_BUCKETS // 2
    nf = jnp.maximum(n, 1).astype(jnp.float32)
    large = max_exact + (jnp.log(nf / max_exact) / math.log(REL_MAX_DIST / max_exact)
                         * (REL_BUCKETS - max_exact)).astype(jnp.int32)
    large = jnp.minimum(large, REL_BUCKETS - 1)
    return jnp.where(n < max_exact, n, large)

def rope_tables(seq_len, dim):
    half = dim // 2
    inv = ROPE_THETA ** (-jnp.arange(half, dtype=jnp.float32) / half)
    ang = jnp.arange(seq_len, dtype=jnp.float32)[:, None] * inv[None, :]
    return jnp.cos(ang), jnp.sin(ang)

def apply_rope(x, cos, sin):
    half = x.shape[-1] // 2
    x1 = x[..., :half].astype(jnp.float32)
    x2 = x[..., half:].astype(jnp.float32)
    return jnp.concatenate([x1 * cos - x2 * sin, x1 * sin + x2 * cos], axis=-1).astype(x.dtype)

def ada_modulate(c, w, b):
    m = jax.nn.silu(c) @ w + b
    shift, scale, gate = jnp.split(m, 3, axis=-1)
    return shift[:, None], scale[:, None], gate[:, None]

def compress(x, pe, w1, b1, w2, b2):
    B_, S_, G_, d = x.shape
    ch = x.reshape(B_, S_ // CMP_STRIDE, CMP_STRIDE, G_, d)
    blk = jnp.concatenate([ch[:, :-1], ch[:, 1:]], axis=2) + pe[None, None, :, None, :]
    nc = blk.shape[1]
    flat = jnp.moveaxis(blk, 3, 2).reshape(B_, nc, G_, CMP_BLOCK * d)
    return jax.nn.gelu(flat @ w1 + b1) @ w2 + b2

def nsa_attention(q, k_cmp, v_cmp, k_slc, v_slc, k_win, v_win, gates, tbl):
    B_, S_, H_, d = q.shape
    G_, hpg = NSA_GROUPS, NSA_HPG
    nc = k_cmp.shape[1]
    ns = S_ // SEL_BLOCK
    n_sel = min(SEL_TOP_N, ns)
    nk_sel = n_sel * SEL_BLOCK
    scale = d ** -0.5
    cmp_start = jnp.arange(nc) * CMP_STRIDE
    cmp_end = cmp_start + CMP_BLOCK - 1
    blk_ids = jnp.arange(ns)
    sel_start = blk_ids * SEL_BLOCK
    overlap = jnp.clip(jnp.minimum(cmp_start[:, None] + CMP_BLOCK, sel_start[None, :] + SEL_BLOCK)
                       - jnp.maximum(cmp_start[:, None], sel_start[None, :]), 0, None
                       ).astype(jnp.float32) / CMP_BLOCK
    ks_blocks = k_slc.reshape(B_, ns, SEL_BLOCK, G_, d).transpose(0, 3, 1, 2, 4)
    vs_blocks = v_slc.reshape(B_, ns, SEL_BLOCK, G_, d).transpose(0, 3, 1, 2, 4)
    kw_pad = jnp.pad(k_win, ((0, 0), (WINDOW, 0), (0, 0), (0, 0)))
    vw_pad = jnp.pad(v_win, ((0, 0), (WINDOW, 0), (0, 0), (0, 0)))
    tbl_heads = tbl.reshape(REL_BUCKETS, G_, hpg)
    tbl_g = tbl_heads.transpose(1, 0, 2)
    b_ix = jnp.arange(B_)[:, None, None, None]
    g_ix = jnp.arange(G_)[None, :, None, None]
    off_blk = jnp.arange(SEL_BLOCK)
    off_win = jnp.arange(Q_BLOCK + WINDOW)

    def block(bi):
        q0 = bi * Q_BLOCK
        t = q0 + jnp.arange(Q_BLOCK)
        qb = lax.dynamic_slice_in_dim(q, q0, Q_BLOCK, axis=1).reshape(B_, Q_BLOCK, G_, hpg, d)
        gb = jax.nn.sigmoid(lax.dynamic_slice_in_dim(gates, q0, Q_BLOCK, axis=1).astype(jnp.float32)
                            ).reshape(B_, Q_BLOCK, G_, hpg, 3)
        dist_c = t[:, None] - cmp_end[None, :]
        bias_c = tbl_heads[t5_bucket(dist_c)].transpose(2, 3, 0, 1)
        s_c = jnp.einsum('bqghd,bkgd->bghqk', qb, k_cmp) * scale + bias_c
        p_c = masked_softmax(s_c, dist_c >= 0)
        o_c = jnp.einsum('bghqk,bkgd->bqghd', p_c.astype(v_cmp.dtype), v_cmp)
        imp = jnp.einsum('bghqk,kn->bgqn', p_c, overlap)
        tb = t // SEL_BLOCK
        forced = (blk_ids[None, :] == 0) | (blk_ids[None, :] == tb[:, None]) | (blk_ids[None, :] == tb[:, None] - 1)
        causal_blk = sel_start[None, :] <= t[:, None]
        score = jnp.where(forced, FORCE, jnp.where(causal_blk, imp, NEG))
        _, idx = lax.top_k(score, n_sel)
        k_g = ks_blocks[b_ix, g_ix, idx].reshape(B_, G_, Q_BLOCK, nk_sel, d)
        v_g = vs_blocks[b_ix, g_ix, idx].reshape(B_, G_, Q_BLOCK, nk_sel, d)
        pos_s = (idx[..., None] * SEL_BLOCK + off_blk).reshape(B_, G_, Q_BLOCK, nk_sel)
        dist_s = t[None, None, :, None] - pos_s
        bias_s = jnp.moveaxis(tbl_g[g_ix, t5_bucket(dist_s)], -1, 2)
        s_s = jnp.einsum('bqghd,bgqkd->bghqk', qb, k_g) * scale + bias_s
        p_s = masked_softmax(s_s, (dist_s >= 0)[:, :, None])
        o_s = jnp.einsum('bghqk,bgqkd->bqghd', p_s.astype(v_g.dtype), v_g)
        kw = lax.dynamic_slice_in_dim(kw_pad, q0, Q_BLOCK + WINDOW, axis=1)
        vw = lax.dynamic_slice_in_dim(vw_pad, q0, Q_BLOCK + WINDOW, axis=1)
        pos_w = q0 - WINDOW + off_win
        dist_w = t[:, None] - pos_w[None, :]
        mask_w = (pos_w[None, :] >= 0) & (dist_w >= 0) & (dist_w < WINDOW)
        bias_w = tbl_heads[t5_bucket(dist_w)].transpose(2, 3, 0, 1)
        s_w = jnp.einsum('bqghd,bkgd->bghqk', qb, kw) * scale + bias_w
        p_w = masked_softmax(s_w, mask_w)
        o_w = jnp.einsum('bghqk,bkgd->bqghd', p_w.astype(vw.dtype), vw)
        o = gb[..., 0:1] * o_c + gb[..., 1:2] * o_s + gb[..., 2:3] * o_w
        return o.reshape(B_, Q_BLOCK, H_ * d).astype(q.dtype)

    out = lax.map(block, jnp.arange(S_ // Q_BLOCK))
    return out.transpose(1, 0, 2, 3).reshape(B_, S_, H_ * d)

def mla_attention(q_nope, q_pe, k_nope, k_pe, v):
    B_, S_, H_, _ = q_nope.shape
    dv = v.shape[-1]
    scale = (MLA_NOPE + MLA_ROPE) ** -0.5
    kpos = jnp.arange(S_)

    def block(bi):
        q0 = bi * Q_BLOCK
        t = q0 + jnp.arange(Q_BLOCK)
        qn = lax.dynamic_slice_in_dim(q_nope, q0, Q_BLOCK, axis=1)
        qr = lax.dynamic_slice_in_dim(q_pe, q0, Q_BLOCK, axis=1)
        s = (jnp.einsum('bqhd,bkhd->bhqk', qn, k_nope) + jnp.einsum('bqhd,bkd->bhqk', qr, k_pe)) * scale
        p = masked_softmax(s, kpos[None, :] <= t[:, None])
        o = jnp.einsum('bhqk,bkhd->bqhd', p.astype(v.dtype), v)
        return o.reshape(B_, Q_BLOCK, H_ * dv)

    out = lax.map(block, jnp.arange(S_ // Q_BLOCK))
    return out.transpose(1, 0, 2, 3).reshape(B_, S_, H_ * dv)

def dsa_attention(q, k, v, iq, ik, iw, tbl):
    B_, S_, H_, d = q.shape
    kvh = k.shape[2]
    hpg = H_ // kvh
    k_sel = min(DSA_TOPK_MAX, S_ // 4)
    scale = d ** -0.5
    kpos = jnp.arange(S_)
    b_ix = jnp.arange(B_)[:, None, None]

    def block(bi):
        q0 = bi * Q_BLOCK
        t = q0 + jnp.arange(Q_BLOCK)
        iqb = lax.dynamic_slice_in_dim(iq, q0, Q_BLOCK, axis=1)
        iwb = lax.dynamic_slice_in_dim(iw, q0, Q_BLOCK, axis=1).astype(jnp.float32)
        rel = jax.nn.relu(jnp.einsum('bqhd,bkd->bqhk', iqb, ik).astype(jnp.float32))
        score = jnp.einsum('bqhk,bqh->bqk', rel, iwb)
        score = jnp.where(kpos[None, None, :] <= t[None, :, None], score, NEG)
        _, idx = lax.top_k(score, k_sel)
        kg = k[b_ix, idx]
        vg = v[b_ix, idx]
        dist = t[None, :, None] - idx
        bias = tbl[t5_bucket(dist)].reshape(B_, Q_BLOCK, k_sel, kvh, hpg).transpose(0, 3, 4, 1, 2)
        qb = lax.dynamic_slice_in_dim(q, q0, Q_BLOCK, axis=1).reshape(B_, Q_BLOCK, kvh, hpg, d)
        s = jnp.einsum('bqghd,bqkgd->bghqk', qb, kg) * scale + bias
        p = masked_softmax(s, (dist >= 0)[:, None, None])
        o = jnp.einsum('bghqk,bqkgd->bqghd', p.astype(vg.dtype), vg)
        return o.reshape(B_, Q_BLOCK, H_ * d)

    out = lax.map(block, jnp.arange(S_ // Q_BLOCK))
    return out.transpose(1, 0, 2, 3).reshape(B_, S_, H_ * d)

def even_mixer(h, rel_bias, w_in, w_out, nsa_qk_g, cmp_pe, cmp_w1, cmp_b1, cmp_w2, cmp_b2,
               mla_q_norm_g, mla_kv_norm_g, mla_w_uq, mla_w_ukv, mla_nope_g, mla_rope_g):
    B_, S_, _ = h.shape
    proj = h @ w_in
    sizes = (NSA_HEADS * HEAD_DIM, 6 * NSA_GROUPS * HEAD_DIM, 3 * NSA_HEADS, MLA_Q_RANK, MLA_KV_RANK, MLA_ROPE)
    q_n, kv_n, gate_n, cq, ckv, kpe = jnp.split(proj, _offsets(sizes), axis=-1)
    q_n = rms_norm(q_n.reshape(B_, S_, NSA_HEADS, HEAD_DIM), nsa_qk_g[0])
    kv_n = kv_n.reshape(B_, S_, 6, NSA_GROUPS, HEAD_DIM)
    k_cmp = rms_norm(compress(kv_n[:, :, 0], cmp_pe[0], cmp_w1[0], cmp_b1[0], cmp_w2[0], cmp_b2[0]), nsa_qk_g[1])
    v_cmp = compress(kv_n[:, :, 1], cmp_pe[1], cmp_w1[1], cmp_b1[1], cmp_w2[1], cmp_b2[1])
    k_slc = rms_norm(kv_n[:, :, 2], nsa_qk_g[1])
    k_win = rms_norm(kv_n[:, :, 4], nsa_qk_g[1])
    gates = gate_n.reshape(B_, S_, NSA_HEADS, 3)
    o_nsa = nsa_attention(q_n, k_cmp, v_cmp, k_slc, kv_n[:, :, 3], k_win, kv_n[:, :, 5], gates,
                          rel_bias[:, :NSA_HEADS])
    qf = (rms_norm(cq, mla_q_norm_g) @ mla_w_uq).reshape(B_, S_, MLA_HEADS, MLA_NOPE + MLA_ROPE)
    kvf = (rms_norm(ckv, mla_kv_norm_g) @ mla_w_ukv).reshape(B_, S_, MLA_HEADS, MLA_NOPE + MLA_V)
    cos, sin = rope_tables(S_, MLA_ROPE)
    q_nope = rms_norm(qf[..., :MLA_NOPE], mla_nope_g[0])
    q_pe = apply_rope(rms_norm(qf[..., MLA_NOPE:], mla_rope_g[0]), cos[:, None], sin[:, None])
    k_nope = rms_norm(kvf[..., :MLA_NOPE], mla_nope_g[1])
    k_pe = apply_rope(rms_norm(kpe, mla_rope_g[1]), cos, sin)
    o_mla = mla_attention(q_nope, q_pe, k_nope, k_pe, kvf[..., MLA_NOPE:])
    return jnp.concatenate([o_nsa, o_mla], axis=-1) @ w_out

def odd_mixer(h, rel_bias, w_in, w_out, qk_g):
    B_, S_, _ = h.shape
    proj = h @ w_in
    sizes = (DSA_HEADS * HEAD_DIM, DSA_KV_HEADS * HEAD_DIM, DSA_KV_HEADS * HEAD_DIM, IDX_HEADS * IDX_DIM, IDX_DIM, IDX_HEADS)
    q, k, v, iq, ik, iw = jnp.split(proj, _offsets(sizes), axis=-1)
    q = rms_norm(q.reshape(B_, S_, DSA_HEADS, HEAD_DIM), qk_g[0])
    k = rms_norm(k.reshape(B_, S_, DSA_KV_HEADS, HEAD_DIM), qk_g[1])
    v = v.reshape(B_, S_, DSA_KV_HEADS, HEAD_DIM)
    cos, sin = rope_tables(S_, IDX_ROPE)
    iq = iq.reshape(B_, S_, IDX_HEADS, IDX_DIM)
    iq = jnp.concatenate([apply_rope(iq[..., :IDX_ROPE], cos[:, None], sin[:, None]), iq[..., IDX_ROPE:]], axis=-1) * (IDX_DIM ** -0.5)
    ik = jnp.concatenate([apply_rope(ik[..., :IDX_ROPE], cos, sin), ik[..., IDX_ROPE:]], axis=-1)
    iw = iw * (IDX_HEADS ** -0.5)
    return dsa_attention(q, k, v, iq, ik, iw, rel_bias) @ w_out

def conv_ffn(h, w_up, conv_w, conv_b, w_down):
    S_ = h.shape[1]
    u = h @ w_up
    up = jnp.pad(u, ((0, 0), (CONV_WIDTH - 1, 0), (0, 0)))
    u = sum(conv_w[j] * up[:, j:j + S_] for j in range(CONV_WIDTH)) + conv_b
    gate, val = jnp.split(u, 2, axis=-1)
    return (jax.nn.silu(gate) * val) @ w_down

def setup_inputs(seed: int = 0) -> dict:
    key = jax.random.key(seed)
    ks = jax.random.split(key, 32)

    def w(k, shape, fan_in, mult=1.0):
        return jax.random.normal(k, shape, jnp.float32) * (mult * fan_in ** -0.5)

    def gain(k, shape):
        return 1.0 + 0.05 * jax.random.normal(k, shape, jnp.float32)

    def bias(k, shape, s=0.02):
        return s * jax.random.normal(k, shape, jnp.float32)

    D = D_MODEL
    return {
        "x": jax.random.normal(ks[0], (BATCH, SEQ, D), jnp.float32),
        "c": jax.random.normal(ks[1], (BATCH, D), jnp.float32),
        "rel_bias": bias(ks[2], (REL_BUCKETS, N_SLOTS), 0.5),
        "ada_w": w(ks[3], (DEPTH, 2, D, 3 * D), D, 0.5),
        "ada_b": bias(ks[4], (DEPTH, 2, 3 * D)),
        "norm_g": gain(ks[5], (DEPTH, 2, D)),
        "ev_w_in": w(ks[6], (N_EVEN, D, EVEN_COLS), D),
        "ev_w_out": w(ks[7], (N_EVEN, EVEN_OUT, D), EVEN_OUT),
        "nsa_qk_g": gain(ks[8], (N_EVEN, 2, HEAD_DIM)),
        "cmp_pe": bias(ks[9], (N_EVEN, 2, CMP_BLOCK, HEAD_DIM), 0.1),
        "cmp_w1": w(ks[10], (N_EVEN, 2, CMP_BLOCK * HEAD_DIM, CMP_HIDDEN), CMP_BLOCK * HEAD_DIM),
        "cmp_b1": bias(ks[11], (N_EVEN, 2, CMP_HIDDEN)),
        "cmp_w2": w(ks[12], (N_EVEN, 2, CMP_HIDDEN, HEAD_DIM), CMP_HIDDEN),
        "cmp_b2": bias(ks[13], (N_EVEN, 2, HEAD_DIM)),
        "mla_q_norm_g": gain(ks[14], (N_EVEN, MLA_Q_RANK)),
        "mla_kv_norm_g": gain(ks[15], (N_EVEN, MLA_KV_RANK)),
        "mla_w_uq": w(ks[16], (N_EVEN, MLA_Q_RANK, MLA_HEADS * (MLA_NOPE + MLA_ROPE)), MLA_Q_RANK),
        "mla_w_ukv": w(ks[17], (N_EVEN, MLA_KV_RANK, MLA_HEADS * (MLA_NOPE + MLA_V)), MLA_KV_RANK),
        "mla_nope_g": gain(ks[18], (N_EVEN, 2, MLA_NOPE)),
        "mla_rope_g": gain(ks[19], (N_EVEN, 2, MLA_ROPE)),
        "od_w_in": w(ks[20], (N_ODD, D, ODD_COLS), D),
        "od_w_out": w(ks[21], (N_ODD, ODD_OUT, D), ODD_OUT),
        "dsa_qk_g": gain(ks[22], (N_ODD, 2, HEAD_DIM)),
        "ffn_w_up": w(ks[23], (DEPTH, D, 2 * FFN_HIDDEN), D),
        "ffn_conv_w": w(ks[24], (DEPTH, CONV_WIDTH, 2 * FFN_HIDDEN), CONV_WIDTH),
        "ffn_conv_b": bias(ks[25], (DEPTH, 2 * FFN_HIDDEN)),
        "ffn_w_down": w(ks[26], (DEPTH, FFN_HIDDEN, D), FFN_HIDDEN),
    }

def reference(x, c, rel_bias, ada_w, ada_b, norm_g, ev_w_in, ev_w_out, nsa_qk_g, cmp_pe, cmp_w1, cmp_b1,
              cmp_w2, cmp_b2, mla_q_norm_g, mla_kv_norm_g, mla_w_uq, mla_w_ukv, mla_nope_g, mla_rope_g,
              od_w_in, od_w_out, dsa_qk_g, ffn_w_up, ffn_conv_w, ffn_conv_b, ffn_w_down):
    for i in range(DEPTH):
        j = i // 2
        shift, scale, gate = ada_modulate(c, ada_w[i, 0], ada_b[i, 0])
        h = rms_norm(x, norm_g[i, 0]) * (1.0 + scale) + shift
        if i % 2 == 0:
            mix = even_mixer(h, rel_bias, ev_w_in[j], ev_w_out[j], nsa_qk_g[j], cmp_pe[j], cmp_w1[j],
                             cmp_b1[j], cmp_w2[j], cmp_b2[j], mla_q_norm_g[j], mla_kv_norm_g[j],
                             mla_w_uq[j], mla_w_ukv[j], mla_nope_g[j], mla_rope_g[j])
        else:
            mix = odd_mixer(h, rel_bias, od_w_in[j], od_w_out[j], dsa_qk_g[j])
        x = x + gate * mix
        shift, scale, gate = ada_modulate(c, ada_w[i, 1], ada_b[i, 1])
        h = rms_norm(x, norm_g[i, 1]) * (1.0 + scale) + shift
        x = x + gate * conv_ffn(h, ffn_w_up[i], ffn_conv_w[i], ffn_conv_b[i], ffn_w_down[i])
    return x


_drawn_inputs = setup_inputs


def setup_inputs(seed=0):
    import zlib

    import numpy as np

    out = dict(_drawn_inputs(seed))
    spreads = {}
    factors = {'nsa_qk_g': 8.0,
     'cmp_pe': 6.564,
     'cmp_b1': 8.0,
     'cmp_b2': 8.0,
     'mla_q_norm_g': 8.0,
     'mla_kv_norm_g': 8.0,
     'mla_nope_g': 8.0,
     'mla_rope_g': 8.0,
     'dsa_qk_g': 8.0,
     'ffn_conv_b': 5.931,
     'rel_bias': 3.278}
    for name, (base, spread) in spreads.items():
        noise = np.random.default_rng([zlib.crc32(name.encode()), seed]).standard_normal(out[name].shape)
        drawn = base * np.exp(spread * noise) if base else spread * noise
        out[name] = jnp.asarray(drawn.astype(out[name].dtype))
    for name, factor in factors.items():
        out[name] = (out[name] * factor).astype(out[name].dtype)
    return out
```

```python
import math
from contextlib import ExitStack, contextmanager

import numpy as np

import concourse.bass as bass
from concourse import mybir

F32 = mybir.dt.float32
ALU = mybir.AluOpType
ACT = mybir.ActivationFunctionType
AX_X = mybir.AxisListType.X

P = 128
D = 2048
S = 256
ST = S // P
KT = D // P
HD = 128
NSA_H, NSA_G, MLA_H, DSA_H, DSA_KV = 8, 2, 8, 16, 4
Q_RANK, KV_RANK, ROPE = 512, 256, 64
IDX_H, IDX_D, IDX_ROPE = 16, 64, 32
BANK_TURNS = (0, 2, 1, 3)
TOPK = min(256, S // 4)
CMP_BLOCK, CMP_STRIDE, CMP_HID = 32, 16, 256
NCMP = S // CMP_STRIDE - 1
FFN = 4096
FT = FFN // P
BUCKETS, SLOTS, MAX_DIST = 32, 16, 128
EPS, NEG = 1e-6, -1e30
TAKEN = -3e38

E_Q, E_KV, E_GATE = 0, NSA_H * HD, NSA_H * HD + 6 * NSA_G * HD
E_CQ = E_GATE + 3 * NSA_H
E_CKV, E_KPE = E_CQ + Q_RANK, E_CQ + Q_RANK + KV_RANK
E_COLS = E_KPE + ROPE
O_K = DSA_H * HD
O_V = O_K + DSA_KV * HD
O_IQ = O_V + DSA_KV * HD
O_IK = O_IQ + IDX_H * IDX_D
O_IW = O_IK + IDX_D
O_COLS = O_IW + IDX_H

NB = 512
UK = 4
RING = 4
UNIT = UK * NB

ROWS = {}
_at = 0
for _name, _n in (("c", KT), ("norm_g", 4 * KT), ("nsa_g", 2), ("dsa_g", 2), ("nope_g", 2),
                  ("qn_g", Q_RANK // P), ("kvn_g", KV_RANK // P), ("b1", 4)):
    ROWS[_name] = (_at, _n)
    _at += _n
ROWS_A = _at
PE_COL = P
CW_COL = 2 * P
CB_COL = CW_COL + 2 * 3 * 2 * FT
PRM = CB_COL + 2 * 2 * FT

C_ID, C_CAUSAL = 0, P
C_CMASK = C_CAUSAL + S
C_VALID = C_CMASK + ST * NCMP
C_COS64 = C_VALID + ST
C_SIN64 = C_COS64 + ST * ROPE // 2
C_COS32 = C_SIN64 + ST * ROPE // 2
C_SIN32 = C_COS32 + ST * IDX_ROPE // 2
C_FLIP = C_SIN32 + ST * IDX_ROPE // 2
C_COLS = C_FLIP + P
REV = 384
FWD0 = S - 1
FWD = 2 * S


def constants():
    t = np.arange(S)
    con = np.zeros((P, C_COLS), np.float32)
    con[:, C_ID:C_ID + P] = np.eye(P, dtype=np.float32)
    con[:, C_CAUSAL:C_CAUSAL + S] = np.where(t[None, :] <= P + np.arange(P)[:, None], 0.0, NEG)
    ends = np.arange(NCMP) * CMP_STRIDE + CMP_BLOCK - 1
    dist = t[:, None] - ends[None, :]
    con[:, C_CMASK:C_VALID] = np.where(dist >= 0, 0.0, NEG).reshape(ST, P, NCMP).transpose(1, 0, 2).reshape(P, -1)
    con[:, C_VALID:C_COS64] = (dist >= 0).any(1).reshape(ST, P).T

    def rope(dim):
        half = dim // 2
        inv = np.float32(10000.0) ** (-np.arange(half, dtype=np.float32) / np.float32(half))
        ang = t.astype(np.float32)[:, None] * inv[None, :]
        lay = lambda a: a.reshape(ST, P, half).transpose(1, 0, 2).reshape(P, -1)
        return lay(np.cos(ang)), lay(np.sin(ang))

    con[:, C_COS64:C_SIN64], con[:, C_SIN64:C_COS32] = rope(ROPE)
    con[:, C_COS32:C_SIN32], con[:, C_SIN32:C_FLIP] = rope(IDX_ROPE)
    con[:, C_FLIP:C_COLS] = np.eye(P, dtype=np.float32)[::-1]

    def bucket(d):
        n = np.maximum(d, 0)
        exact = BUCKETS // 2
        nf = np.maximum(n, 1).astype(np.float32)
        large = exact + (np.log(nf / np.float32(exact)) / np.float32(math.log(MAX_DIST / exact))
                         * np.float32(BUCKETS - exact)).astype(np.int32)
        return np.where(n < exact, n, np.minimum(large, BUCKETS - 1))

    hot = np.zeros((BUCKETS, REV + FWD), np.float32)
    j = np.arange(REV)
    hot[bucket(S - 1 - j), j] = 1.0
    d = np.arange(FWD) - FWD0
    hot[bucket(d), REV + np.arange(FWD)] = 1.0
    negrow = np.broadcast_to(np.where(j < S, 0.0, NEG).astype(np.float32), (SLOTS, REV))
    return {"k_con": con, "k_hot": hot, "k_neg": np.ascontiguousarray(negrow)}


class Signal:

    def __init__(self, handle):
        self.handle, self.n = handle, 0


class Lane:

    def __init__(self, eng):
        self.eng, self.last = eng, None

    def done(self, ins, sig):
        ins.then_inc(sig.handle, 1)
        sig.n = sig.n + 1
        self.last = (sig, sig.n)

    def after(self):
        if self.last is not None:
            self.eng.wait_ge(self.last[0].handle, self.last[1])

    @contextmanager
    def loop(self, start, end, per, tail):
        base = {s: s.n for s in per}
        assert base[tail] > 0
        self.after()
        with self.eng.Fori(start, end) as i:
            for s, k in per.items():
                s.n = base[s] + (i - start) * k
            self.last = (tail, tail.n)
            yield i
        for s, k in per.items():
            s.n = base[s] + k * (end - start)
        self.last = (tail, tail.n)


def weight_plan():
    at, plan = 0, {}
    for name, n in (("ev_in", 28), ("cmp", 8), ("uq", 3), ("ukv", 2), ("ev_out", 16), ("up0", 64), ("down0", 32),
                    ("od_in", 36), ("od_out", 16), ("up1", 64), ("down1", 32)):
        plan[name] = at
        at += n
    return plan


def trunk_program(nc, x, c, rel_bias, ada_w, ada_b, norm_g, ev_w_in, ev_w_out, nsa_qk_g, cmp_pe, cmp_w1, cmp_b1,
                  cmp_w2, cmp_b2, mla_q_norm_g, mla_kv_norm_g, mla_w_uq, mla_w_ukv, mla_nope_g, mla_rope_g,
                  od_w_in, od_w_out, dsa_qk_g, ffn_w_up, ffn_conv_w, ffn_conv_b, ffn_w_down,
                  k_con, k_hot, k_neg, out):
    PLAN = weight_plan()
    ctx = ExitStack()
    with ctx:
        def sb(name, shape):
            return ctx.enter_context(nc.sbuf_tensor(name, shape, F32))

        def sem(name):
            return ctx.enter_context(nc.semaphore(name))

        def sig(name):
            return Signal(sem(name))

        x_sb = sb("x_sb", [P, ST, D])
        hT = sb("hT", [P, KT, S])
        wide = sb("wide", [P, ST * O_COLS])
        side = sb("side", [P, 7168])
        bias = sb("bias", [P, SLOTS, S])
        acc = sb("acc", [P, 3, D])
        aring = sb("aring", [P, 2, D])
        ring = sb("ring", [P, RING, UNIT])
        con = sb("con", [P, C_COLS])
        prm = sb("prm", [P, PRM])
        ropeg = sb("ropeg", [P, 2 * ROPE])
        ones = sb("ones", [P, P])
        cs = sb("cs", [P, KT])
        cs_now = sb("cs_now", [P, 4])
        cw_now = sb("cw_now", [P, 4, 2, 8])
        modc = sb("modc", [P, 2, KT])
        xst = sb("xst", [P, 2])
        st = sb("st", [P, 64])
        kT = sb("kT", [P, 4, S])
        kpT = sb("kpT", [ROPE, S])
        qT = sb("qT", [P, 2, S])
        knT = sb("knT", [P, 2, S])
        qpT = sb("qpT", [ROPE, 2, S])
        L = sb("L", [P, 3, 3 * P])
        PT = sb("PT", [P, 2, 3 * P])
        mx = sb("mx", [P, 3, 2])
        nmx = sb("nmx", [P, 3, 2])
        sm = sb("sm", [P, 3, 2])
        rw = sb("rw", [P, 3, 2])
        cbias = sb("cbias", [P, ST, NCMP, NSA_H])
        gs = sb("gs", [P, 3])
        ps = ctx.enter_context(nc.psum_tensor("ps", [P, 8, 512], F32))
        toeplitz = nc.dram_tensor("toeplitz", (SLOTS, REV), F32, kind="Internal").ap()

        ident = con[:, C_ID:C_ID + P]
        causal = con[:, C_CAUSAL:C_CAUSAL + S]
        valid = con[:, C_VALID:C_VALID + ST]
        act_sb = wide[:, 0:FT * S].rearrange("p (f s) -> p f s", f=FT)
        ev = wide[:, 0:ST * E_COLS].rearrange("p (t n) -> p t n", t=ST)
        od = wide[:, 0:ST * O_COLS].rearrange("p (t n) -> p t n", t=ST)
        xn = side[:, 0:ST * D].rearrange("p (t n) -> p t n", t=ST)
        KVF = MLA_H * 2 * HD
        QF = MLA_H * (HD + ROPE)
        kvf = side[:, 0:ST * KVF].rearrange("p (t n) -> p t n", t=ST)
        qf = side[:, ST * KVF:ST * (KVF + QF)].rearrange("p (t n) -> p t n", t=ST)
        flat = side[:, 0:2 * CMP_BLOCK * 30].rearrange("p (a l r) -> p a l r", a=2, l=CMP_BLOCK)
        cbuf = side[:, 0:1024].rearrange("p (b g s) -> p b g s", b=2, g=2)
        sgate = side[:, 1024:1536].rearrange("p (b s) -> p b s", b=2)
        rtmp = side[:, 1536:2560].rearrange("p (b s) -> p b s", b=2)
        rows = side[:, 4096:4096 + 6 * P].rearrange("p (r n) -> p r n", r=6)
        rev = side[0:SLOTS, 5120:5120 + REV]
        negrow = side[0:SLOTS, 5632:5632 + REV]
        hot = side[0:BUCKETS, 6016:6016 + REV + FWD]
        tbl = side[0:BUCKETS, 6912:6912 + SLOTS]
        tail = ST * E_COLS
        w2 = wide[:, tail:tail + 512].rearrange("p (a k n) -> p a k n", a=2, k=2)
        b2 = wide[0:1, tail + 512:tail + 768]
        kc = wide[0:NCMP, tail + 768:tail + 1024]
        vc = wide[0:NCMP, tail + 1024:tail + 1280]
        hid = wide[:, tail + 1280:tail + 1400].rearrange("p (a k r) -> p a k r", a=2, k=2)
        kcT = wide[:, tail + 1400:tail + 1400 + NSA_G * NCMP]
        hotr, hotf = hot[:, 0:REV], hot[:, REV:REV + FWD]
        iqT = side[:, 0:512].rearrange("p (b s) -> p b s", b=2)
        ikT = side[:, 512:768]
        ikd = side[:, 768:1024].rearrange("p (t n) -> p t n", t=ST)
        rel = side[:, 1024:1024 + 768].rearrange("p (b s) -> p b s", b=2)
        isc = side[:, 1792:1792 + 384]
        iwk = side[:, 2176:2176 + 384]
        selm = side[:, 2560:2560 + 384]
        m8 = side[:, 2944:2952]
        scr = side[:, 3072:7168]

        msq = PT[:, 0, 0:HD]

        params_in = sem("params_in")
        x_in = sem("x_in")
        rows_in = sem("rows_in")
        landed = [sem(f"landed{s}") for s in range(RING)]
        ada_landed = [sem(f"ada_landed{s}") for s in range(2)]
        toep_out, toep_in, out_stored = sem("toep_out"), sem("toep_in"), sem("out_stored")
        acc_bias = sem("acc_bias")
        unit_used = sig("unit_used")
        pe_s, act_s, dve_s, pool_s = sig("pe_s"), sig("act_s"), sig("dve_s"), sig("pool_s")
        ada_used = sig("ada_used")
        acc_clear = sig("acc_clear")
        cols_done = sig("cols_done")
        prm_T = sig("prm_T")
        prm_ok = sig("prm_ok")
        cs_ok, ones_ok = sig("cs_ok"), sig("ones_ok")
        modc_ok = sig("modc_ok")
        xsq, xsd, xn_ok = sig("xsq"), sig("xsd"), sig("xn_ok")
        xT = sig("xT")
        hT_act, hT_dve = sig("hT_act"), sig("hT_dve")
        proj_out = sig("proj_out")
        gate_red, gate_ok = sig("gate_red"), sig("gate_ok")
        res_out = sig("res_out")
        up_conv, up_silu, up_pair = sig("up_conv"), sig("up_silu"), sig("up_pair")
        cw_ok, gconv = sig("cw_ok"), sig("gconv")
        rev_mm, rev_ok, cb_mm, cb_ok = sig("rev_mm"), sig("rev_ok"), sig("cb_mm"), sig("cb_ok")

        (ev_sq, ev_var, ev_nrm, gates_raw, gates_ok, ek_T, ek_ok, flat_ok, hid_ok, kc_T, kc_sq, kc_var, kc_ok, kcT_ok,
         vc_ok, mla_out, ukv_mm, mla_sq, mla_var, mla_nrm) = (sig(n) for n in (
             "ev_sq", "ev_var", "ev_nrm", "gates_raw", "gates_ok", "ek_T", "ek_ok", "flat_ok", "hid_ok", "kc_T", "kc_sq",
             "kc_var", "kc_ok", "kcT_ok", "vc_ok", "mla_out", "ukv_mm", "mla_sq", "mla_var", "mla_nrm"))
        (od_sq, od_var, od_nrm, dk_T, dk_ok, irope, iq_T, iq_ok, idx_mm, irel, isum) = (sig(n) for n in (
            "od_sq", "od_var", "od_nrm", "dk_T", "dk_ok", "irope", "iq_T", "iq_ok", "idx_mm", "irel", "isum"))

        flipped, bias_ok = sig("flipped"), sig("bias_ok")

        block = ctx.enter_context(nc.Block())

        def wsrc(w, k0, kn, c0, n):
            return w[k0 * P:(k0 + kn) * P, c0:c0 + n] if isinstance(c0, int) else w[k0 * P:(k0 + kn) * P, bass.ds(c0, n)]

        n_params = [0]

        @block.sync
        def _(sp):
            def row_load(r, at, src):
                n = src.shape[0]
                sp.dma_start(rows[at:at + n, r, :], src).then_inc(rows_in, 16)
                n_params[0] += 1

            row_load(0, ROWS["c"][0], c.rearrange("o (k p) -> (o k) p", p=P))
            row_load(0, ROWS["norm_g"][0], norm_g.rearrange("i j (k p) -> (i j k) p", p=P))
            row_load(0, ROWS["nsa_g"][0], nsa_qk_g.rearrange("o g p -> (o g) p"))
            row_load(0, ROWS["dsa_g"][0], dsa_qk_g.rearrange("o g p -> (o g) p"))
            row_load(0, ROWS["nope_g"][0], mla_nope_g.rearrange("o g p -> (o g) p"))
            row_load(0, ROWS["qn_g"][0], mla_q_norm_g.rearrange("o (k p) -> (o k) p", p=P))
            row_load(0, ROWS["kvn_g"][0], mla_kv_norm_g.rearrange("o (k p) -> (o k) p", p=P))
            row_load(0, ROWS["b1"][0], cmp_b1.rearrange("o g (k p) -> (o g k) p", p=P))
            row_load(1, 0, cmp_pe.rearrange("o g l p -> (o g l) p"))
            cw = ffn_conv_w.rearrange("l j (k p) -> (l j k) p", p=P)
            for r in range(3):
                row_load(2 + r, 0, cw[r * P:(r + 1) * P, :])
            row_load(5, 0, ffn_conv_b.rearrange("l (k p) -> (l k) p", p=P))
            for dst, src in ((con[:, :], k_con), (hot, k_hot), (negrow, k_neg), (tbl, rel_bias),
                             (w2, cmp_w2.rearrange("o g (k p) n -> p (o g) k n", p=P)),
                             (b2, cmp_b2.rearrange("o g n -> o (g n)")),
                             (ropeg[:, :], bass.AP(mla_rope_g.tensor, 0, [[0, P], [1, 2 * ROPE]]))):
                sp.dma_start(dst, src).then_inc(params_in, 16)
            sp.dma_start(x_sb[:, :, :], x.rearrange("o (t p) n -> p (o t) n", p=P)).then_inc(x_in, 16)

            def unit(idx, u, src, dst):
                if not (isinstance(idx, int) and idx < RING):
                    sp.wait_ge(unit_used.handle, idx - (RING - 1))
                sp.dma_start(dst, src).then_inc(landed[u % RING], 16)

            def matrix(first, w, units, c0, n, idx_extra=0):
                for u in range(units):
                    g = first + u
                    src = wsrc(w, u * UK, UK, c0, n).rearrange("(k p) n -> p k n", p=P)
                    dst = ring[:, g % RING, 0:UK * n].rearrange("p (k n) -> p k n", k=UK)
                    unit(g + idx_extra, g, src, dst)

            matrix(0, ev_w_in[0], 4, 0, NB)
            matrix(4, ev_w_in[0], 4, NB, NB)
            with sp.Fori(1, 3) as i:
                for b in range(2):
                    matrix(4 * b, ev_w_in[0], 4, i * (2 * NB) + b * NB, NB, i * 8)
            matrix(24, ev_w_in[0], 4, 6 * NB, E_COLS - 6 * NB)
            for a in range(2):
                w1 = cmp_w1[0, a].rearrange("(l p) n -> p l n", p=P)
                for u in range(4):
                    g = PLAN["cmp"] + 4 * a + u
                    unit(g, g, w1[:, 8 * u:8 * u + 8, :], ring[:, g % RING, :].rearrange("p (l n) -> p l n", l=8))
            for b in range(3):
                matrix(PLAN["uq"] + b, mla_w_uq[0], 1, b * NB, NB)
            for b in range(2):
                g = PLAN["ukv"] + b
                unit(g, g, mla_w_ukv[0].rearrange("(k p) n -> p k n", p=P)[:, :, b * 1024:(b + 1) * 1024],
                     ring[:, g % RING, :].rearrange("p (k n) -> p k n", k=2))

            def narrow(name, w, units):
                with sp.Fori(0, 2) as i:
                    for b in range(2):
                        matrix(PLAN[name] + units * b, w, units, i * (2 * NB) + b * NB, NB, i * (2 * units))

            def up(name, w):
                with sp.Fori(0, 4) as i:
                    for s in range(2):
                        for gv in range(2):
                            matrix(PLAN[name] + 8 * s + 4 * gv, w, 4, i * (2 * NB) + (s * NB + gv * FFN), NB, i * 16)

            narrow("ev_out", ev_w_out[0], 4)
            up("up0", ffn_w_up[0])
            narrow("down0", ffn_w_down[0], 8)
            with sp.Fori(0, 4) as i:
                for b in range(2):
                    matrix(PLAN["od_in"] + 4 * b, od_w_in[0], 4, i * (2 * NB) + b * NB, NB, i * 8)
            matrix(PLAN["od_in"] + 32, od_w_in[0], 4, 8 * NB, O_COLS - 8 * NB)
            narrow("od_out", od_w_out[0], 4)
            up("up1", ffn_w_up[1])
            narrow("down1", ffn_w_down[1], 8)
            for b in range(4):
                sp.wait_ge(res_out.handle, 3 * 4 + b + 1)
                sp.dma_start(out.rearrange("o (t p) n -> p (o t) n", p=P)[:, :, b * NB:(b + 1) * NB],
                             x_sb[:, :, b * NB:(b + 1) * NB]).then_inc(out_stored, 16)
            sp.wait_ge(out_stored, 64)

        GROUPS = [(-1, (0, 1)), (0, (2, 0, 1)), (1, (2, 0, 1)), (2, (2, 0, 1)), (3, (2,))]

        def sub_of(g, third):
            return g if third == 2 else g + 1

        def first_ada(g):
            return {-1: 0, 0: 32, 1: 80, 2: 128, 3: 176}[g]

        @block.gpsimd
        def _(pool):
            lane = Lane(pool)
            lane.done(nc.gpsimd.memset(ones[:, :], 1.0), ones_ok)
            n_bias = 0
            for g, thirds in GROUPS:
                if g >= 0:
                    if len(thirds) > 1:
                        pool.wait_ge(cols_done.handle, g + 1)
                    if g > 0:
                        pool.wait_ge(res_out.handle, 4 * g)
                for t in thirds:
                    lane.done(nc.gpsimd.memset(acc[:, t, :], 0.0), acc_clear)
                lane.after()
                for t in thirds:
                    n = sub_of(g, t)
                    pool.dma_start(acc[0:1, t, :], ada_b[n // 2, n % 2:n % 2 + 1, t * D:(t + 1) * D]).then_inc(acc_bias, 16)
                    n_bias += 1
                k = len(thirds)
                per = 2 * k

                def units(i, skip=0):
                    for j in range(per):
                        kk, t = divmod(j, k)
                        n = sub_of(g, thirds[t])
                        m = first_ada(g) + j
                        if not (isinstance(i, int) and m < 2):
                            pool.wait_ge(ada_used.handle, i * per + (m - 1))
                        row = i * (2 * P) + kk * P
                        w = ada_w[n // 2, n % 2]
                        src = w[row:row + P, thirds[t] * D:(thirds[t] + 1) * D] if isinstance(row, int) \
                            else w[bass.ds(row, P), thirds[t] * D:(thirds[t] + 1) * D]
                        pool.dma_start(aring[:, j % 2, :], src).then_inc(ada_landed[j % 2], 16)

                if g < 0:
                    units(0)
                    with pool.Fori(1, KT // 2) as i:
                        units(i)
                else:
                    with pool.Fori(0, KT // 2) as i:
                        units(i)

        EV_UNITS = []
        for h in range(NSA_H):
            EV_UNITS += [("cmp", h), ("slc", h), ("win", h)]
        EV_UNITS += [("mla", h) for h in range(MLA_H)]
        OD_UNITS = [("dsa", h) for h in range(DSA_H)]

        def qheads(units):
            n, res, last = -1, [], None
            for kind, h in units:
                key = (kind == "mla", h)
                if key != last:
                    n, last = n + 1, key
                res.append(n)
            return res

        class Att:

            def __init__(self, tag, units):
                self.units, self.qh = units, qheads(units)
                self.q_raw, self.q_ok = sig(f"{tag}_q_raw"), sig(f"{tag}_q_ok")
                self.s_ok = sig(f"{tag}_s_ok")
                self.l_ok = sig(f"{tag}_l_ok")
                self.p_ok = sig(f"{tag}_p_ok")
                self.w_ok = sig(f"{tag}_w_ok")
                self.t_ok, self.pt_ok = sig(f"{tag}_t_ok"), sig(f"{tag}_pt_ok")
                self.o_ok, self.o_out = sig(f"{tag}_o_ok"), sig(f"{tag}_o_out")
                self.last_of = [n for n in range(len(units)) if n + 1 == len(units) or self.qh[n + 1] != self.qh[n]]
                self.first_of = [0] + [n + 1 for n in self.last_of[:-1]]

        EVA, ODA = Att("ev", EV_UNITS), Att("od", OD_UNITS)
        LAG = 2
        S_B, T_B, O_B, Q_B = 0, 2, 4, 6

        def q_cols(att, n):
            kind, h = att.units[n]
            if kind == "dsa":
                return [od[:, t, h * HD:(h + 1) * HD] for t in range(ST)]
            if kind == "mla":
                return [qf[:, t, h * (HD + ROPE):h * (HD + ROPE) + HD] for t in range(ST)]
            return [ev[:, t, E_Q + h * HD:E_Q + (h + 1) * HD] for t in range(ST)]

        def kv_col(which, g):
            return E_KV + (which * NSA_G + g) * HD

        def pe_attention(pe, lane, att):
            units, qh = att.units, att.qh

            def queries(n):
                if n >= len(units) or n not in att.first_of:
                    return
                q = qh[n]
                b = q % 2
                kind, h = units[n]
                if q >= (1 if kind == "mla" else 2):
                    pe.wait_ge(att.q_ok.handle, q if kind == "mla" else q - 1)
                if kind == "mla":
                    for t in range(ST):
                        nc.tensor.transpose(ps[0:ROPE, Q_B + 1, t * P:(t + 1) * P],
                                            qf[:, t, h * (HD + ROPE) + HD:(h + 1) * (HD + ROPE)], ident)
                    for t in range(ST):
                        nc.tensor.transpose(ps[:, Q_B, S + t * P:S + (t + 1) * P], kvf[:, t, h * 2 * HD:h * 2 * HD + HD], ident)
                    b = 0
                for t, col in enumerate(q_cols(att, n)):
                    ins = nc.tensor.transpose(ps[:, Q_B + b, t * P:(t + 1) * P], col, ident)
                lane.done(ins, att.q_raw)

            def logits(n):
                q, b = qh[n], S_B + n % 2
                kind, h = units[n]
                pe.wait_ge(att.q_ok.handle, q + 1)
                if n >= 2:
                    pe.wait_ge(att.l_ok.handle, n - 1)
                qs = qT[:, q % 2, :]
                if kind == "cmp":
                    g = h // (NSA_H // NSA_G)
                    for t in range(ST):
                        ins = nc.tensor.matmul(ps[:, b, t * P:t * P + NCMP], qs[:, t * P:(t + 1) * P],
                                               kcT[:, g * NCMP:(g + 1) * NCMP], start=True, stop=True)
                else:
                    for t, off, nk in ((1, 0, S), (0, S, P)):
                        parts = []
                        if kind == "mla":
                            parts = [(qs[:, t * P:(t + 1) * P], knT[:, q % 2, 0:nk]),
                                     (qpT[:, q % 2, t * P:(t + 1) * P], kpT[:, 0:nk])]
                        else:
                            k = {"slc": h // 4, "win": 2 + h // 4, "dsa": h // 4}[kind]
                            parts = [(qs[:, t * P:(t + 1) * P], kT[:, k, 0:nk])]
                        for j, (l, r) in enumerate(parts):
                            ins = nc.tensor.matmul(ps[:, b, off:off + nk], l, r, start=j == 0, stop=j == len(parts) - 1)
                lane.done(ins, att.s_ok)

            def output(n):
                kind, h = units[n]
                b = T_B + n % 2
                pe.wait_ge(att.w_ok.handle, n + 1)
                if n >= 2:
                    pe.wait_ge(att.pt_ok.handle, n - 1)
                p = L[:, n % 3, :]
                if kind == "cmp":
                    for t in range(ST):
                        ins = nc.tensor.transpose(ps[0:NCMP, b, t * P:(t + 1) * P], p[:, t * NCMP:(t + 1) * NCMP], ident)
                else:
                    nc.tensor.transpose(ps[:, b, 0:P], p[:, S:S + P], ident)
                    nc.tensor.transpose(ps[:, b, P:2 * P], p[:, 0:P], ident)
                    ins = nc.tensor.transpose(ps[:, b, 2 * P:3 * P], p[:, P:2 * P], ident)
                lane.done(ins, att.t_ok)

            def values(n):
                kind, h = units[n]
                q = qh[n]
                first, last = n in att.first_of, n in att.last_of
                if first and q >= 2:
                    pe.wait_ge(att.o_out.handle, q - 1)
                pe.wait_ge(att.pt_ok.handle, n + 1)
                o = ps[:, O_B + q % 2, 0:S]
                g = h // 4
                if kind == "cmp":
                    ins = nc.tensor.matmul(o, vc[:, g * HD:(g + 1) * HD], PT[0:NCMP, n % 2, 0:S], start=first, stop=last)
                else:
                    v = {"slc": lambda t: ev[:, t, kv_col(3, g):kv_col(3, g) + HD],
                         "win": lambda t: ev[:, t, kv_col(5, g):kv_col(5, g) + HD],
                         "mla": lambda t: kvf[:, t, h * 2 * HD + HD:(h + 1) * 2 * HD],
                         "dsa": lambda t: od[:, t, O_V + g * HD:O_V + (g + 1) * HD]}[kind]
                    late = ps[:, O_B + q % 2, P:S]
                    if first:
                        nc.tensor.matmul(late, v(1), PT[:, n % 2, 2 * P:3 * P], start=True, stop=False)
                        nc.tensor.matmul(late, v(0), PT[:, n % 2, P:S], start=False, stop=True)
                        ins = nc.tensor.matmul(ps[:, O_B + q % 2, 0:P], v(0), PT[:, n % 2, 0:P], start=True, stop=True)
                    else:
                        nc.tensor.matmul(late, v(1), PT[:, n % 2, 2 * P:3 * P], start=False, stop=False)
                        ins = nc.tensor.matmul(o, v(0), PT[:, n % 2, 0:S], start=False, stop=last)
                lane.done(ins, att.o_ok)

            queries(0)
            for n in range(len(units) + LAG + 1):
                queries(n + 1)
                if n < len(units):
                    logits(n)
                if 0 <= n - LAG < len(units):
                    output(n - LAG)
                if 0 <= n - LAG - 1 < len(units):
                    values(n - LAG - 1)

        @block.tensor
        def _(pe):
            lane = Lane(pe)

            def wait_unit(u, extra=0):
                pe.wait_ge(landed[u % RING], extra * 4 + 16 * (u // RING + 1))

            pe.wait_ge(rows_in, 16 * n_params[0])
            pe.wait_ge(params_in, 16 * 7)
            for r, (n, at) in enumerate(((ROWS_A, 0), (2 * CMP_BLOCK, PE_COL), (P, CW_COL), (P, CW_COL + P),
                                         (P, CW_COL + 2 * P), (P, CB_COL))):
                ins = nc.tensor.transpose(ps[:, r // 4, (r % 4) * P:(r % 4) * P + n], rows[0:n, r, :], con[0:n, C_ID:C_ID + n])
            lane.done(ins, prm_T)
            ins = nc.tensor.matmul(ps[0:SLOTS, 2, 0:REV], tbl[:, :], hotr, start=True, stop=True)
            lane.done(ins, rev_mm)
            for t in range(ST):
                for j in range(NCMP):
                    d0 = FWD0 + t * P - CMP_STRIDE * j - (CMP_BLOCK - 1)
                    ins = nc.tensor.matmul(ps[:, 3, (t * NCMP + j) * NSA_H:(t * NCMP + j + 1) * NSA_H],
                                           hotf[:, d0:d0 + P], tbl[:, 0:NSA_H], start=True, stop=True)
            lane.done(ins, cb_mm)

            pe.wait_ge(toep_in, 16)
            pe.wait_ge(prm_ok.handle, 4)
            pe.wait_ge(cb_ok.handle, 1)
            for b in range(8):
                ins = nc.tensor.matmul(ps[:, b, :], con[:, C_FLIP:C_FLIP + P], wide[:, b * 512:(b + 1) * 512], start=True, stop=True)
            lane.done(ins, flipped)
            pe.wait_ge(bias_ok.handle, 8)

            def modulation(n):
                pe.wait_ge(ones_ok.handle, 1)
                pe.wait_ge(ada_used.handle, first_ada(n - 1) + (32 if n == 0 else 48))
                for t in range(2):
                    for j in range(KT):
                        ins = nc.tensor.matmul(ps[:, 7, t * KT + j:t * KT + j + 1], acc[:, t, j * P:(j + 1) * P], ones[:, 0:1],
                                               start=True, stop=True)
                lane.done(ins, cols_done)

            def normed(n):
                pe.wait_ge(xn_ok.handle, 2 * (n + 1))
                for b in range(8):
                    if b == 3:
                        pe.wait_ge(modc_ok.handle, 2 * (n + 1))
                    if b >= 4:
                        pe.wait_ge((hT_act if b % 2 == 0 else hT_dve).handle, 8 * n + 2 * ((b - 4) // 2 + 1))
                    for k in range(2):
                        for t in range(ST):
                            ins = nc.tensor.transpose(ps[:, 4 + b % 4, k * S + t * P:k * S + (t + 1) * P],
                                                      xn[:, t, (2 * b + k) * P:(2 * b + k + 1) * P], ident)
                    lane.done(ins, xT)
                pe.wait_ge(hT_act.handle, 8 * (n + 1))
                pe.wait_ge(hT_dve.handle, 8 * (n + 1))

            def rows_block(first, units, n, bank, left, extra=0):
                for u in range(units):
                    g = first + u
                    wait_unit(g, extra)
                    w = ring[:, g % RING, 0:UK * n].rearrange("p (k n) -> p k n", k=UK)
                    for k in range(UK):
                        for t in range(ST):
                            ins = nc.tensor.matmul(ps[:, bank + t, 0:n], left(u * UK + k)[:, t * P:(t + 1) * P], w[:, k, :],
                                                   start=(u == 0 and k == 0), stop=(u == units - 1 and k == UK - 1))
                    lane.done(ins, unit_used)

            def in_proj(name, pairs, cols, seen):
                rows_block(PLAN[name], 4, NB, 0, lambda k: hT[:, k, :])
                rows_block(PLAN[name] + 4, 4, NB, 2, lambda k: hT[:, k, :])
                base = unit_used.n
                with pe.Fori(1, pairs) as i:
                    for b in range(2):
                        pe.wait_ge(proj_out.handle, i * 2 + (seen + b - 1))
                        rows_block(PLAN[name] + 4 * b, 4, NB, 2 * b, lambda k: hT[:, k, :], i * 8)
                unit_used.n = base + (pairs - 1) * 8
                pe.wait_ge(proj_out.handle, seen + 2 * pairs - 1)
                rows_block(PLAN[name] + 8 * pairs, 4, cols - 2 * pairs * NB, 0, lambda k: hT[:, k, :])

            def gate_rows(n):
                pe.wait_ge(ada_used.handle, first_ada(n) + (48 if n < 3 else 16))
                for j in range(4):
                    ins = nc.tensor.matmul(ps[:, 4 + j, :], ones[:, :], acc[:, 2, j * NB:(j + 1) * NB], start=True, stop=True)
                lane.done(ins, gate_red)

            def out_side(name, n, units, left):
                gate_rows(n)
                for b in range(2):
                    rows_block(PLAN[name] + units * b, units, NB, 2 * b, left)
                for b in range(2):
                    pe.wait_ge(res_out.handle, 4 * n + 1 + b)
                    rows_block(PLAN[name] + units * (2 + b), units, NB, 2 * b, left)

            def up(name, f):
                def one_pass(i):
                    for s in range(2):
                        if f > 0 or not isinstance(i, int):
                            pe.wait_ge(up_pair.handle, i * 8 + (32 * f + 4 * s - 4))
                        for gv in range(2):
                            for u in range(4):
                                g = PLAN[name] + 8 * s + 4 * gv + u
                                wait_unit(g, i * 16)
                                w = ring[:, g % RING, :].rearrange("p (k n) -> p k n", k=UK)
                                for k in range(UK):
                                    for q in range(4):
                                        ins = nc.tensor.matmul(
                                            ps[:, 4 * s + 2 * gv + q // 2, (q % 2) * S:(q % 2 + 1) * S],
                                            w[:, k, q * P:(q + 1) * P], hT[:, u * UK + k, :],
                                            start=(u == 0 and k == 0 and q % 2 == 0), stop=(u == 3 and k == UK - 1),
                                            skip_group_check=True)
                                lane.done(ins, unit_used)
                one_pass(0)
                with lane.loop(1, 4, {unit_used: 16}, unit_used) as i:
                    one_pass(i)

            def even_mixer():
                pe.wait_ge(ev_nrm.handle, 14)
                for j, (which, g) in enumerate(((2, 0), (2, 1), (4, 0), (4, 1))):
                    for t in range(ST):
                        ins = nc.tensor.transpose(ps[:, 4 + j // 2, (j % 2) * S + t * P:(j % 2) * S + (t + 1) * P],
                                                  ev[:, t, kv_col(which, g):kv_col(which, g) + HD], ident)
                lane.done(ins, ek_T)
                for a in range(2):
                    for g in range(NSA_G):
                        for t in range(ST):
                            ins = nc.tensor.transpose(ps[:, 6 + a, g * S + t * P:g * S + (t + 1) * P],
                                                      ev[:, t, kv_col(a, g):kv_col(a, g) + HD], ident)
                lane.done(ins, ek_T)
                for b in range(3):
                    if b < 2:
                        pe.wait_ge(ek_ok.handle, b + 1)
                    else:
                        pe.wait_ge(flat_ok.handle, 4)
                    for k in range(2):
                        col = (E_CQ + (2 * b + k) * P) if b < 2 else E_CKV + k * P
                        for t in range(ST):
                            ins = nc.tensor.transpose(ps[:, 4 + b, k * S + t * P:k * S + (t + 1) * P], ev[:, t, col:col + P], ident)
                    lane.done(ins, ek_T)
                pe.wait_ge(flat_ok.handle, 8)
                for t in range(ST):
                    ins = nc.tensor.transpose(ps[0:ROPE, 7, t * P:(t + 1) * P], ev[:, t, E_KPE:E_KPE + ROPE], ident)
                lane.done(ins, ek_T)
                for a in range(2):
                    for u in range(4):
                        g = PLAN["cmp"] + 4 * a + u
                        wait_unit(g)
                        w = ring[:, g % RING, :].rearrange("p (l n) -> p l n", l=8)
                        for l in range(8):
                            for hc in range(2):
                                ins = nc.tensor.matmul(ps[:, 2 * a + hc, 0:NSA_G * NCMP], w[:, l, hc * P:(hc + 1) * P],
                                                       flat[:, a, 8 * u + l, :], start=(u == 0 and l == 0), stop=(u == 3 and l == 7))
                        lane.done(ins, unit_used)
                pe.wait_ge(ek_ok.handle, 9)
                pe.wait_ge(hid_ok.handle, 4)
                for a in range(2):
                    for g in range(NSA_G):
                        o = ps[0:NCMP, 4 + a, g * HD:(g + 1) * HD]
                        for hc in range(2):
                            nc.tensor.matmul(o, hid[:, a, hc, g * NCMP:(g + 1) * NCMP], w2[:, a, hc, :], start=hc == 0, stop=False)
                        ins = nc.tensor.matmul(o, ones[0:1, 0:NCMP], b2[0:1, a * HD:(a + 1) * HD], start=False, stop=True)
                lane.done(ins, kc_T)
                for b in range(7):
                    bank = 2 * (b % 2)
                    if b >= 2:
                        pe.wait_ge(mla_out.handle, b - 1)
                    if b < 3:
                        rows_block(PLAN["uq"] + b, 1, NB, bank, lambda k: hT[:, 8 + k, :])
                    else:
                        g = PLAN["ukv"] + (b - 3) // 2
                        if b % 2 == 1:
                            wait_unit(g)
                        w = ring[:, g % RING, :].rearrange("p (k n) -> p k n", k=2)
                        for k in range(2):
                            for t in range(ST):
                                ins = nc.tensor.matmul(ps[:, bank + t, :], hT[:, 12 + k, t * P:(t + 1) * P],
                                                       w[:, k, ((b - 3) % 2) * NB:((b - 3) % 2 + 1) * NB], start=k == 0, stop=k == 1)
                        lane.done(ins, ukv_mm)
                        if b % 2 == 0:
                            pe.wait_ge(ukv_mm.handle, b - 2)
                            lane.done(pe.nop(), unit_used)
                pe.wait_ge(kc_ok.handle, 2)
                for g in range(NSA_G):
                    ins = nc.tensor.transpose(ps[:, 6, g * NCMP:(g + 1) * NCMP], kc[:, g * HD:(g + 1) * HD], con[0:NCMP, C_ID:C_ID + NCMP])
                lane.done(ins, kc_T)
                pe.wait_ge(kcT_ok.handle, 1)
                pe.wait_ge(vc_ok.handle, 1)
                pe.wait_ge(mla_nrm.handle, 10)
                pe.wait_ge(gates_ok.handle, 1)
                pe_attention(pe, lane, EVA)
                pe.wait_ge(EVA.o_out.handle, NSA_H + MLA_H)

            def odd_mixer():
                pe.wait_ge(od_nrm.handle, 4)
                for j in range(DSA_KV):
                    for t in range(ST):
                        ins = nc.tensor.transpose(ps[:, 4 + j // 2, (j % 2) * S + t * P:(j % 2) * S + (t + 1) * P],
                                                  od[:, t, O_K + j * HD:O_K + (j + 1) * HD], ident)
                lane.done(ins, dk_T)
                pe.wait_ge(irope.handle, 3)
                for t in range(ST):
                    ins = nc.tensor.transpose(ps[:, 6, t * P:(t + 1) * P], ikd[:, t, :], ident)
                lane.done(ins, dk_T)

                def pair_T(p):
                    if p >= 2:
                        pe.wait_ge(iq_ok.handle, p - 1)
                    for t in range(ST):
                        ins = nc.tensor.transpose(ps[:, p % 2, t * P:(t + 1) * P], od[:, t, O_IQ + p * P:O_IQ + (p + 1) * P], ident)
                    lane.done(ins, iq_T)

                pair_T(0)
                pe.wait_ge(dk_ok.handle, 3)
                for p in range(IDX_H // 2):
                    if p + 1 < IDX_H // 2:
                        pair_T(p + 1)
                    pe.wait_ge(iq_ok.handle, p + 1)
                    for e in range(2):
                        hh = 2 * p + e
                        if hh >= 4:
                            pe.wait_ge(irel.handle, hh - 3)
                        r = slice(e * IDX_D, (e + 1) * IDX_D)
                        nc.tensor.matmul(ps[:, 2 + hh % 4, 0:S], iqT[r, p % 2, P:2 * P], ikT[r, 0:S], start=True, stop=True)
                        ins = nc.tensor.matmul(ps[:, 2 + hh % 4, S:S + P], iqT[r, p % 2, 0:P], ikT[r, 0:P], start=True, stop=True)
                        lane.done(ins, idx_mm)
                pe.wait_ge(irel.handle, IDX_H)
                pe_attention(pe, lane, ODA)
                pe.wait_ge(ODA.o_out.handle, DSA_H)

            for n in range(4):
                if n > 0:
                    pe.wait_ge(gate_ok.handle, 4 * n)
                modulation(n)
                normed(n)
                if n == 0:
                    in_proj("ev_in", 3, E_COLS, 0)
                    even_mixer()
                    out_side("ev_out", n, 4, lambda k: hT[:, k, :])
                elif n == 2:
                    in_proj("od_in", 4, O_COLS, 7)
                    odd_mixer()
                    out_side("od_out", n, 4, lambda k: hT[:, k, :])
                else:
                    up(f"up{n // 2}", n // 2)
                    pe.wait_ge(up_pair.handle, 32 * (n // 2 + 1))
                    out_side(f"down{n // 2}", n, 8, lambda k: act_sb[:, k, :])

        @block.scalar
        def _(act):
            lane = Lane(act)

            def run(sig_, out_, in_, f, chain=False, **kw):
                if chain:
                    lane.after()
                ins = nc.scalar.activation(out_, in_, f, **kw)
                if sig_ is not None:
                    lane.done(ins, sig_)

            act.wait_ge(prm_ok.handle, 4)
            run(cs_ok, cs[:, :], prm[:, ROWS["c"][0]:ROWS["c"][0] + KT], ACT.Silu)
            act.wait_ge(rev_ok.handle, 1)
            act.dma_start(toeplitz, rev).then_inc(toep_out, 16)
            act.wait_ge(toep_out, 16)
            act.dma_start(wide[:, 0:SLOTS * S].rearrange("p (h s) -> p h s", h=SLOTS),
                          bass.AP(toeplitz.tensor, 0, [[1, P], [REV, SLOTS], [1, S]])).then_inc(toep_in, 16)
            act.wait_ge(flipped.handle, 1)
            for b in range(8):
                run(bias_ok, bias[:, 2 * b:2 * b + 2, :], ps[:, b, :].rearrange("p (h s) -> p h s", h=2), ACT.Copy)

            def normed(n):
                if n == 0:
                    act.wait_ge(x_in, 16)
                else:
                    act.wait_ge(res_out.handle, 4 * n)
                for t in range(ST):
                    run(xsq, xn[:, t, :], x_sb[:, t, :], ACT.Square, scale=D ** -0.5, accum_out=xst[:, t:t + 1])
                act.wait_ge(xsd.handle, 2 * n + 1)
                run(xsq, xst[:, :], xst[:, :], ACT.Sqrt)
                act.wait_ge(modc_ok.handle, 2 * (n + 1))
                for b in range(0, 8, 2):
                    act.wait_ge(xT.handle, 8 * n + b + 1)
                    for k in range(2):
                        kt = 2 * b + k
                        run(hT_act, hT[:, kt, :], ps[:, 4 + b % 4, k * S:(k + 1) * S], ACT.Identity,
                            bias=modc[:, 0, kt:kt + 1], scale=modc[:, 1, kt:kt + 1])

            def proj(name, pairs, cols, dst):
                def blk(unit_end, bank, c0, n):
                    act.wait_ge(unit_used.handle, unit_end)
                    for t in range(ST):
                        d = dst[:, t, c0:c0 + n] if isinstance(c0, int) else dst[:, t, bass.ds(c0, n)]
                        run(proj_out if t == 1 else None, d, ps[:, bank + t, 0:n], ACT.Copy)
                with act.Fori(0, pairs) as i:
                    base = proj_out.n
                    for b in range(2):
                        blk(i * 8 + (PLAN[name] + 4 * b + 4), 2 * b, i * (2 * NB) + b * NB, NB)
                proj_out.n = base + 2 * pairs
                lane.last = (proj_out, proj_out.n)
                blk(PLAN[name] + 8 * pairs + 4, 0, 2 * pairs * NB, cols - 2 * pairs * NB)

            def gate_copy(n):
                act.wait_ge(gate_red.handle, n + 1)
                for j in range(4):
                    run(gate_ok, acc[:, 2, j * NB:(j + 1) * NB], ps[:, 4 + j, :], ACT.Copy)

            def squares(sig_, col, src, width):
                run(sig_, scr[:, 0:width], src, ACT.Square, chain=True, scale=width ** -0.5, accum_out=st[:, col:col + 1])

            def attention(att):
                units, qh = att.units, att.qh

                def queries(n):
                    if n >= len(units) or n not in att.first_of:
                        return
                    q = qh[n]
                    kind, h = units[n]
                    act.wait_ge(att.q_raw.handle, q + 1)
                    if q >= 2:
                        act.wait_ge(att.s_ok.handle, att.last_of[q - 2] + 1)
                    bank = Q_B if kind == "mla" else Q_B + q % 2
                    if kind == "mla":
                        run(None, qpT[:, q % 2, :], ps[0:ROPE, Q_B + 1, 0:S], ACT.Copy, scale=(HD + ROPE) ** -0.5)
                        run(None, knT[:, q % 2, :], ps[:, Q_B, S:2 * S], ACT.Copy, scale=prm[:, ROWS["nope_g"][0] + 1:ROWS["nope_g"][0] + 2])
                    g = {"dsa": 1, "mla": 2}.get(kind, 0)
                    run(att.q_ok, qT[:, q % 2, :], ps[:, bank, 0:S], ACT.Copy, scale=gs[:, g:g + 1])

                def exps(n):
                    kind, h = units[n]
                    act.wait_ge(att.l_ok.handle, n + 1)
                    for t, off, nk in ((1, 0, S), (0, S, P)):
                        if kind == "cmp":
                            off, nk = t * NCMP, NCMP
                        run(att.p_ok if t == 0 else None, L[:, n % 3, off:off + nk], L[:, n % 3, off:off + nk], ACT.Exp,
                            bias=nmx[:, n % 3, t:t + 1], accum_out=sm[:, n % 3, t:t + 1])

                def probs(n):
                    kind, h = units[n]
                    act.wait_ge(att.t_ok.handle, n + 1)
                    if n >= 2:
                        act.wait_ge(att.o_ok.handle, n - 1)
                    if kind == "cmp":
                        run(att.pt_ok, PT[0:NCMP, n % 2, 0:S], ps[0:NCMP, T_B + n % 2, 0:S], ACT.Copy)
                    else:
                        run(att.pt_ok, PT[:, n % 2, :], ps[:, T_B + n % 2, 0:3 * P], ACT.Copy)

                queries(0)
                for n in range(len(units) + LAG):
                    queries(n + 1)
                    if n < len(units):
                        exps(n)
                    if n >= LAG:
                        probs(n - LAG)

            def even_mixer():
                for t in range(ST):
                    c0 = 15 * t
                    for h in range(NSA_H):
                        squares(ev_sq, c0 + h, ev[:, t, E_Q + h * HD:E_Q + (h + 1) * HD], HD)
                    for j, (w, g) in enumerate(((2, 0), (2, 1), (4, 0), (4, 1))):
                        squares(ev_sq, c0 + 8 + j, ev[:, t, kv_col(w, g):kv_col(w, g) + HD], HD)
                    squares(ev_sq, c0 + 12, ev[:, t, E_CQ:E_CQ + Q_RANK], Q_RANK)
                    squares(ev_sq, c0 + 13, ev[:, t, E_CKV:E_CKV + KV_RANK], KV_RANK)
                    squares(ev_sq, c0 + 14, ev[:, t, E_KPE:E_KPE + ROPE], ROPE)
                act.wait_ge(ev_var.handle, 1)
                run(ev_sq, st[:, 0:30], st[:, 0:30], ACT.Sqrt)
                run(gates_raw, ev[:, :, E_GATE:E_GATE + 3 * NSA_H], ev[:, :, E_GATE:E_GATE + 3 * NSA_H], ACT.Sigmoid)
                act.wait_ge(ek_T.handle, 1)
                for b in range(2):
                    run(ek_ok, kT[:, 2 * b:2 * b + 2, :], ps[:, 4 + b, :].rearrange("p (k s) -> p k s", k=2), ACT.Copy,
                        scale=prm[:, ROWS["nsa_g"][0] + 1:ROWS["nsa_g"][0] + 2])
                for b in range(3):
                    act.wait_ge(ek_T.handle, 3 + b)
                    for k in range(2):
                        col = ROWS["qn_g"][0] + 2 * b + k
                        run(ek_ok, hT[:, 8 + 2 * b + k, :], ps[:, 4 + b, k * S:(k + 1) * S], ACT.Copy, scale=prm[:, col:col + 1])
                act.wait_ge(ek_T.handle, 6)
                run(ek_ok, kpT[:, :], ps[0:ROPE, 7, 0:S], ACT.Copy)
                for a in range(2):
                    act.wait_ge(unit_used.handle, PLAN["cmp"] + 4 * (a + 1))
                    for hc in range(2):
                        col = ROWS["b1"][0] + 2 * a + hc
                        run(hid_ok, hid[:, a, hc, :], ps[:, 2 * a + hc, 0:NSA_G * NCMP], ACT.Gelu_apprx_tanh, bias=prm[:, col:col + 1])
                act.wait_ge(kc_T.handle, 1)
                for g in range(NSA_G):
                    run(kc_sq, scr[0:NCMP, g * HD:(g + 1) * HD], ps[0:NCMP, 4, g * HD:(g + 1) * HD], ACT.Square, scale=HD ** -0.5,
                        accum_out=st[0:NCMP, 60 + g:61 + g])
                act.wait_ge(kc_var.handle, 1)
                run(kc_sq, st[0:NCMP, 60:62], st[0:NCMP, 60:62], ACT.Sqrt)
                for b in range(7):
                    if b < 3:
                        act.wait_ge(unit_used.handle, PLAN["uq"] + b + 1)
                    else:
                        act.wait_ge(ukv_mm.handle, b - 2)
                    for t in range(ST):
                        d = qf[:, t, b * NB:(b + 1) * NB] if b < 3 else kvf[:, t, (b - 3) * NB:(b - 2) * NB]
                        run(mla_out if t == 1 else None, d, ps[:, 2 * (b % 2) + t, :], ACT.Copy)
                lane.after()
                for t in range(ST):
                    for h in range(MLA_H):
                        q0 = h * (HD + ROPE)
                        for j, (src, wd) in enumerate(((qf[:, t, q0:q0 + HD], HD), (qf[:, t, q0 + HD:q0 + HD + ROPE], ROPE),
                                                       (kvf[:, t, h * 2 * HD:h * 2 * HD + HD], HD))):
                            run(mla_sq, msq[:, 0:wd], src, ACT.Square, chain=True, scale=wd ** -0.5,
                                accum_out=st[:, 24 * t + 8 * j + h:24 * t + 8 * j + h + 1])
                act.wait_ge(mla_var.handle, 1)
                run(mla_sq, st[:, 0:48], st[:, 0:48], ACT.Sqrt)
                act.wait_ge(kc_T.handle, 2)
                run(kcT_ok, kcT, ps[:, 6, 0:NSA_G * NCMP], ACT.Copy, scale=prm[:, ROWS["nsa_g"][0] + 1:ROWS["nsa_g"][0] + 2])
                attention(EVA)

            def odd_mixer():
                for t in range(ST):
                    for h in range(DSA_H + DSA_KV):
                        squares(od_sq, 20 * t + h, od[:, t, h * HD:(h + 1) * HD], HD)
                act.wait_ge(od_var.handle, 1)
                run(od_sq, st[:, 0:40], st[:, 0:40], ACT.Sqrt)
                act.wait_ge(dk_T.handle, 1)
                for b in range(2):
                    run(dk_ok, kT[:, 2 * b:2 * b + 2, :], ps[:, 4 + b, :].rearrange("p (k s) -> p k s", k=2), ACT.Copy,
                        scale=prm[:, ROWS["dsa_g"][0] + 1:ROWS["dsa_g"][0] + 2])
                act.wait_ge(dk_T.handle, 2)
                run(dk_ok, ikT, ps[:, 6, 0:S], ACT.Copy)
                for p in range(IDX_H // 2):
                    act.wait_ge(iq_T.handle, p + 1)
                    if p >= 2:
                        act.wait_ge(idx_mm.handle, 2 * p - 2)
                    run(iq_ok, iqT[:, p % 2, :], ps[:, p % 2, 0:S], ACT.Copy)
                    for e in range(2):
                        hh = 2 * p + e
                        act.wait_ge(idx_mm.handle, hh + 1)
                        if hh >= 2:
                            act.wait_ge(isum.handle, hh - 1)
                        run(irel, rel[:, hh % 2, :], ps[:, 2 + hh % 4, 0:3 * P], ACT.Relu)
                attention(ODA)

            def up(name, f):
                def one_pass(i):
                    act.wait_ge(cw_ok.handle, i * 2 + (8 * f + 2))
                    for s in range(2):
                        act.wait_ge(unit_used.handle, i * 16 + (PLAN[name] + 8 * s + 8))
                        for r, q in enumerate(BANK_TURNS):
                            b = r % 2
                            if not (f == 0 and s == 0 and r < 2 and isinstance(i, int)):
                                act.wait_ge(up_pair.handle, i * 8 + (32 * f + 4 * s + r - 1))
                            for gv in range(2):
                                run(up_conv if gv == 1 else None, cbuf[:, b, gv, :],
                                    ps[:, 4 * s + 2 * gv + q // 2, (q % 2) * S:(q % 2 + 1) * S], ACT.Identity,
                                    bias=cw_now[:, 3, gv, 4 * s + q:4 * s + q + 1], scale=cw_now[:, 2, gv, 4 * s + q:4 * s + q + 1])
                            act.wait_ge(gconv.handle, i * 8 + (32 * f + 4 * s + r + 1))
                            run(up_silu, sgate[:, b, :], cbuf[:, b, 0, :], ACT.Silu)
                one_pass(0)
                with lane.loop(1, 4, {up_conv: 8, up_silu: 8}, up_silu) as i:
                    one_pass(i)

            for n in range(4):
                normed(n)
                if n == 0:
                    proj("ev_in", 3, E_COLS, ev)
                    even_mixer()
                elif n == 2:
                    proj("od_in", 4, O_COLS, od)
                    odd_mixer()
                else:
                    up(f"up{n // 2}", n // 2)
                gate_copy(n)

        @block.vector
        def _(dve):
            lane = Lane(dve)
            v = nc.vector

            def put(ins, sig_=None):
                lane.done(ins, sig_ if sig_ is not None else dve_s)

            dve.wait_ge(prm_T.handle, 1)
            for a, b in ((0, ROWS_A), (PE_COL, PE_COL + 2 * CMP_BLOCK), (CW_COL, 4 * P), (4 * P, PRM)):
                put(v.tensor_copy(prm[:, a:b], ps[:, a // 512, a % 512:a % 512 + b - a]), prm_ok)
            dve.wait_ge(rev_mm.handle, 1)
            put(v.tensor_tensor(rev, ps[0:SLOTS, 2, 0:REV], negrow, ALU.add), rev_ok)
            dve.wait_ge(cb_mm.handle, 1)
            put(v.tensor_tensor(cbias[:, :, :, :].rearrange("p t j h -> p (t j) h"),
                                ps[:, 3, 0:ST * NCMP * NSA_H].rearrange("p (a h) -> p a h", h=NSA_H),
                                con[:, C_CMASK:C_VALID].unsqueeze(2).broadcast_to([P, ST * NCMP, NSA_H]), ALU.add), cb_ok)
            lane.after()
            for j, (name, sc) in enumerate((("nsa_g", HD ** -0.5), ("dsa_g", HD ** -0.5), ("nope_g", (HD + ROPE) ** -0.5))):
                put(v.tensor_scalar(gs[:, j:j + 1], prm[:, ROWS[name][0]:ROWS[name][0] + 1], sc, None, ALU.mult))
            dve.wait_ge(cs_ok.handle, 1)

            def ada_unit(j, thirds, m0, extra, col):
                m = m0 + j
                dve.wait_ge(ada_landed[m % 2], extra * 8 + 16 * (m // 2 + 1))
                lane.after()
                t = thirds[j % len(thirds)]
                put(v.scalar_tensor_tensor(acc[:, t, :], aring[:, m % 2, :], col, acc[:, t, :], ALU.mult, ALU.add), ada_used)

            def ada_group(g, thirds):
                dve.wait_ge(acc_clear.handle, {-1: 2, 0: 5, 1: 8, 2: 11, 3: 12}[g])
                dve.wait_ge(acc_bias, 16 * {-1: 2, 0: 5, 1: 8, 2: 11, 3: 12}[g])
                k = len(thirds)
                with lane.loop(0, KT // 2, {ada_used: 2 * k, dve_s: 1}, ada_used) if ada_used.n > 0 else first_loop(k) as i:
                    lane.after()
                    put(v.tensor_copy(cs_now[:, 0:2], cs[:, bass.ds(i * 2, 2)]))
                    for j in range(2 * k):
                        ada_unit(j, thirds, first_ada(g), i * (2 * k), cs_now[:, j // k:j // k + 1])

            @contextmanager
            def first_loop(k):
                put(v.tensor_copy(cs_now[:, 0:2], cs[:, 0:2]))
                for j in range(2 * k):
                    ada_unit(j, (0, 1), 0, 0, cs_now[:, j // k:j // k + 1])
                with lane.loop(1, KT // 2, {ada_used: 2 * k, dve_s: 1}, ada_used) as i:
                    yield i

            def normed(n):
                dve.wait_ge(xsq.handle, 3 * n + 2)
                put(v.tensor_scalar(xst[:, :], xst[:, :], EPS, None, ALU.add), xsd)
                dve.wait_ge(xsq.handle, 3 * n + 3)
                put(v.reciprocal(xst[:, :], xst[:, :]), xsd)
                lane.after()
                put(v.tensor_scalar(xn[:, 0, :], x_sb[:, 0, :], xst[:, 0:1], None, ALU.mult), xn_ok)
                put(v.tensor_scalar(xn[:, 1, :], x_sb[:, 1, :], xst[:, 1:2], None, ALU.mult), xn_ok)

            def modulate(n):
                dve.wait_ge(cols_done.handle, n + 1)
                put(v.tensor_copy(modc[:, 0, :], ps[:, 7, 0:KT]), modc_ok)
                g0 = ROWS["norm_g"][0] + n * KT
                put(v.scalar_tensor_tensor(modc[:, 1, :], ps[:, 7, KT:2 * KT], 1.0, prm[:, g0:g0 + KT], ALU.add, ALU.mult), modc_ok)
                lane.after()
                for b in range(1, 8, 2):
                    dve.wait_ge(xT.handle, 8 * n + b + 1)
                    for k in range(2):
                        kt = 2 * b + k
                        put(v.tensor_scalar(hT[:, kt, :], ps[:, 4 + b % 4, k * S:(k + 1) * S], modc[:, 1, kt:kt + 1],
                                            modc[:, 0, kt:kt + 1], ALU.mult, ALU.add), hT_dve)

            def residual(name, n, units):
                dve.wait_ge(gate_ok.handle, 4 * (n + 1))
                for b in range(4):
                    dve.wait_ge(unit_used.handle, PLAN[name] + units * (b + 1))
                    cols = slice(b * NB, (b + 1) * NB)
                    lane.after()
                    for t in range(ST):
                        put(v.tensor_tensor(rtmp[:, t, :], ps[:, 2 * (b % 2) + t, :], acc[:, 2, cols], ALU.mult))
                    lane.after()
                    ins0 = v.tensor_tensor(x_sb[:, 0, cols], x_sb[:, 0, cols], rtmp[:, 0, :], ALU.add)
                    put(ins0)
                    put(v.tensor_tensor(x_sb[:, 1, cols], x_sb[:, 1, cols], rtmp[:, 1, :], ALU.add), res_out)

            def rotate(x1, x2, cos, sin, tmp, sig_):
                a, b, c_, d_ = tmp
                lane.after()
                put(v.tensor_tensor(a, x1, cos, ALU.mult))
                put(v.tensor_tensor(b, x2, sin, ALU.mult))
                put(v.tensor_tensor(c_, x1, sin, ALU.mult))
                put(v.tensor_tensor(d_, x2, cos, ALU.mult))
                lane.after()
                put(v.tensor_tensor(x1, a, b, ALU.subtract))
                put(v.tensor_tensor(x2, c_, d_, ALU.add), sig_)

            def scale_heads(x3, r, heads, sig_):
                put(v.tensor_tensor(x3, x3, r.unsqueeze(2).broadcast_to([P, heads, x3.shape[2]]), ALU.mult), sig_)

            def attention(att, out_slot):
                units, qh = att.units, att.qh

                def logits(n):
                    kind, h = units[n]
                    dve.wait_ge(att.s_ok.handle, n + 1)
                    if n >= 3:
                        dve.wait_ge(att.t_ok.handle, n - 2)
                    lane.after()
                    src = ps[:, S_B + n % 2, :]
                    l = L[:, n % 3, :]
                    for t, off, nk in ((1, 0, S), (0, S, P)):
                        if kind == "cmp":
                            i0, o, b = src[:, t * P:t * P + NCMP], l[:, t * NCMP:(t + 1) * NCMP], cbias[:, t, :, h]
                        else:
                            i0, o = src[:, off:off + nk], l[:, off:off + nk]
                            b0 = 0 if t == 1 else P
                            b = causal[:, b0:S] if kind == "mla" else bias[:, h, b0:S]
                        if kind == "dsa":
                            put(v.tensor_tensor(o, i0, selm[:, off:off + nk], ALU.add))
                            lane.after()
                            i0 = o
                        put(v.tensor_tensor_reduce(o, i0, b, 1.0, TAKEN, ALU.add, ALU.max, mx[:, n % 3, t:t + 1]))
                    lane.after()
                    put(v.tensor_scalar(nmx[:, n % 3, :], mx[:, n % 3, :], -1.0, None, ALU.mult), att.l_ok)

                def weights(n):
                    kind, h = units[n]
                    dve.wait_ge(att.p_ok.handle, n + 1)
                    lane.after()
                    put(v.reciprocal(rw[:, n % 3, :], sm[:, n % 3, :]))
                    lane.after()
                    if kind in ("cmp", "slc", "win"):
                        col = E_GATE + 3 * h + ("cmp", "slc", "win").index(kind)
                        put(v.tensor_tensor(rw[:, n % 3, :], rw[:, n % 3, :], ev[:, :, col], ALU.mult))
                        lane.after()
                    for t, off, nk in ((1, 0, S), (0, S, P)):
                        if kind == "cmp":
                            off, nk = t * NCMP, NCMP
                        p = L[:, n % 3, off:off + nk]
                        put(v.tensor_scalar(p, p, rw[:, n % 3, t:t + 1], None, ALU.mult), att.w_ok if t == 0 else None)

                def output(n):
                    if n not in att.last_of:
                        return
                    q = qh[n]
                    dve.wait_ge(att.o_ok.handle, n + 1)
                    put(v.tensor_copy(hT[:, q, :], ps[:, O_B + q % 2, 0:S]), att.o_out)

                for n in range(len(units) + 5):
                    if n < len(units):
                        logits(n)
                    if 0 <= n - 1 < len(units):
                        weights(n - 1)
                    if 0 <= n - 4 < len(units):
                        output(n - 4)

            def even_mixer():
                dve.wait_ge(ev_sq.handle, 30)
                put(v.tensor_scalar(st[:, 0:30], st[:, 0:30], EPS, None, ALU.add), ev_var)
                dve.wait_ge(ev_sq.handle, 31)
                put(v.reciprocal(st[:, 0:30], st[:, 0:30]))
                lane.after()
                for t in range(ST):
                    r = st[:, 15 * t:15 * t + 15]
                    hd = lambda c0, k: ev[:, t, c0:c0 + k * HD].rearrange("p (h d) -> p h d", h=k)
                    scale_heads(hd(E_Q, NSA_H), r[:, 0:8], 8, ev_nrm)
                    scale_heads(hd(kv_col(2, 0), 2), r[:, 8:10], 2, ev_nrm)
                    scale_heads(hd(kv_col(4, 0), 2), r[:, 10:12], 2, ev_nrm)
                    for c0, wd, k in ((E_CQ, Q_RANK, 12), (E_CKV, KV_RANK, 13)):
                        put(v.tensor_scalar(ev[:, t, c0:c0 + wd], ev[:, t, c0:c0 + wd], r[:, k:k + 1], None, ALU.mult), ev_nrm)
                    put(v.scalar_tensor_tensor(ev[:, t, E_KPE:E_KPE + ROPE], ev[:, t, E_KPE:E_KPE + ROPE], r[:, 14:15],
                                               ropeg[:, ROPE:2 * ROPE], ALU.mult, ALU.mult), ev_nrm)
                H2 = ROPE // 2
                for t in range(ST):
                    cos, sin = (con[:, c0 + t * H2:c0 + (t + 1) * H2] for c0 in (C_COS64, C_SIN64))
                    rotate(ev[:, t, E_KPE:E_KPE + H2], ev[:, t, E_KPE + H2:E_KPE + ROPE], cos, sin,
                           [scr[:, j * H2:(j + 1) * H2] for j in range(4)], ev_nrm)
                dve.wait_ge(ek_T.handle, 2)
                for a in range(2):
                    for g in range(NSA_G):
                        for hh in range(2):
                            src = ps[:, 6 + a, g * S + 16 * hh:g * S + 16 * hh + 240].rearrange("p (j l) -> p j l", l=16)
                            dst = flat[:, a, 16 * hh:16 * hh + 16, g * NCMP:(g + 1) * NCMP].rearrange("p l j -> p j l")
                            pe_ = prm[:, PE_COL + a * 32 + 16 * hh:PE_COL + a * 32 + 16 * hh + 16]
                            put(v.tensor_tensor(dst, src, pe_.unsqueeze(1).broadcast_to([P, NCMP, 16]), ALU.add), flat_ok)
                dve.wait_ge(gates_raw.handle, 1)
                gc = ev[:, :, E_GATE:E_GATE + 3 * NSA_H].rearrange("p t (h c) -> p t h c", c=3)[:, :, :, 0]
                put(v.tensor_tensor(gc, gc, valid.unsqueeze(2).broadcast_to([P, ST, NSA_H]), ALU.mult), gates_ok)
                dve.wait_ge(kc_sq.handle, 2)
                put(v.tensor_scalar(st[0:NCMP, 60:62], st[0:NCMP, 60:62], EPS, None, ALU.add), kc_var)
                put(v.tensor_copy(vc[:, :], ps[0:NCMP, 5, 0:NSA_G * HD]), vc_ok)
                dve.wait_ge(kc_sq.handle, 3)
                put(v.reciprocal(st[0:NCMP, 60:62], st[0:NCMP, 60:62]))
                lane.after()
                for g in range(NSA_G):
                    put(v.tensor_scalar(kc[:, g * HD:(g + 1) * HD], ps[0:NCMP, 4, g * HD:(g + 1) * HD], st[0:NCMP, 60 + g:61 + g],
                                        None, ALU.mult), kc_ok)
                dve.wait_ge(mla_sq.handle, 48)
                put(v.tensor_scalar(st[:, 0:48], st[:, 0:48], EPS, None, ALU.add), mla_var)
                dve.wait_ge(mla_sq.handle, 49)
                put(v.reciprocal(st[:, 0:48], st[:, 0:48]))
                lane.after()
                for t in range(ST):
                    q3 = qf[:, t, :].rearrange("p (h d) -> p h d", h=MLA_H)
                    k3 = kvf[:, t, :].rearrange("p (h d) -> p h d", h=MLA_H)
                    r = st[:, 24 * t:24 * t + 24]
                    scale_heads(q3[:, :, 0:HD], r[:, 0:8], MLA_H, mla_nrm)
                    scale_heads(q3[:, :, HD:HD + ROPE], r[:, 8:16], MLA_H, mla_nrm)
                    scale_heads(k3[:, :, 0:HD], r[:, 16:24], MLA_H, mla_nrm)
                    lane.after()
                    put(v.tensor_tensor(q3[:, :, HD:HD + ROPE], q3[:, :, HD:HD + ROPE],
                                        ropeg[:, 0:ROPE].unsqueeze(1).broadcast_to([P, MLA_H, ROPE]), ALU.mult), mla_nrm)
                    cos, sin = (con[:, c0 + t * H2:c0 + (t + 1) * H2].unsqueeze(1).broadcast_to([P, MLA_H, H2])
                                for c0 in (C_COS64, C_SIN64))
                    tmp = [L[:, :, :].rearrange("p b s -> p (b s)")[:, j * 256:(j + 1) * 256].rearrange("p (h d) -> p h d", h=MLA_H)
                           for j in range(4)]
                    rotate(q3[:, :, HD:HD + H2], q3[:, :, HD + H2:HD + ROPE], cos, sin, tmp, mla_nrm)
                dve.wait_ge(bias_ok.handle, 8)
                attention(EVA, None)

            def odd_mixer():
                Hf = IDX_ROPE // 2
                dve.wait_ge(proj_out.handle, 16)
                for t in range(ST):
                    iq3 = od[:, t, O_IQ:O_IK].rearrange("p (h d) -> p h d", h=IDX_H)
                    c1, s1 = (con[:, c0 + t * Hf:c0 + (t + 1) * Hf] for c0 in (C_COS32, C_SIN32))
                    c3, s3 = (a.unsqueeze(1).broadcast_to([P, IDX_H, Hf]) for a in (c1, s1))
                    tmp = [scr[:, 2048 + j * 256:2048 + (j + 1) * 256].rearrange("p (h d) -> p h d", h=IDX_H) for j in range(4)]
                    rotate(iq3[:, :, 0:Hf], iq3[:, :, Hf:2 * Hf], c3, s3, tmp, None)
                    ik = od[:, t, O_IK:O_IW]
                    rotate(ik[:, 0:Hf], ik[:, Hf:2 * Hf], c1, s1, [scr[:, 3072 + j * Hf:3072 + (j + 1) * Hf] for j in range(4)], None)
                lane.after()
                put(v.tensor_scalar(od[:, :, O_IW:O_COLS], od[:, :, O_IW:O_COLS], IDX_H ** -0.5 * IDX_D ** -0.5, None, ALU.mult), irope)
                for e in range(2):
                    put(v.tensor_copy(ikd[:, :, e * IDX_D:(e + 1) * IDX_D], od[:, :, O_IK:O_IW]), irope)
                dve.wait_ge(od_sq.handle, 40)
                put(v.tensor_scalar(st[:, 0:40], st[:, 0:40], EPS, None, ALU.add), od_var)
                dve.wait_ge(od_sq.handle, 41)
                put(v.reciprocal(st[:, 0:40], st[:, 0:40]))
                lane.after()
                for t in range(ST):
                    scale_heads(od[:, t, O_K:O_V].rearrange("p (h d) -> p h d", h=DSA_KV), st[:, 20 * t + 16:20 * t + 20], DSA_KV, od_nrm)
                for t in range(ST):
                    scale_heads(od[:, t, 0:O_K].rearrange("p (h d) -> p h d", h=DSA_H), st[:, 20 * t:20 * t + 16], DSA_H, od_nrm)
                for hh in range(IDX_H):
                    dve.wait_ge(irel.handle, hh + 1)
                    lane.after()
                    for t, off, nk in ((1, 0, S), (0, S, P)):
                        w = od[:, t, O_IW + hh:O_IW + hh + 1]
                        r = rel[:, hh % 2, off:off + nk]
                        o = isc[:, off:off + nk]
                        if hh == 0:
                            ins = v.tensor_scalar(o, r, w, None, ALU.mult)
                        else:
                            ins = v.scalar_tensor_tensor(o, r, w, o, ALU.mult, ALU.add)
                        put(ins, isum if t == 0 else None)
                lane.after()
                for t, off, nk in ((1, 0, S), (0, S, P)):
                    o = isc[:, off:off + nk]
                    put(v.tensor_tensor(o, o, causal[:, S - nk:S], ALU.add))
                for t, off, nk in ((1, 0, S), (0, S, P)):
                    cur = isc[:, off:off + nk]
                    work = iwk[:, off:off + nk]
                    for r in range(TOPK // 8):
                        lane.after()
                        put(v.max(m8, cur))
                        lane.after()
                        put(v.match_replace(work, m8, cur, TAKEN))
                        cur = work
                lane.after()
                put(v.tensor_scalar(selm, iwk, TAKEN / 2, NEG, ALU.is_gt, ALU.mult))
                attention(ODA, None)

            def up(name, f):
                n = 2 * f + 1
                thirds = (2, 0, 1) if n < 3 else (2,)
                k = 4 * len(thirds)
                cw4 = prm[:, CW_COL + f * 6 * FT:CW_COL + (f + 1) * 6 * FT].rearrange("p (j g t) -> p j g t", j=3, g=2)
                cb3 = prm[:, CB_COL + f * 2 * FT:CB_COL + (f + 1) * 2 * FT].rearrange("p (g t) -> p g t", g=2)
                count = {1: 8, 3: 12}[n]
                dve.wait_ge(acc_clear.handle, count)
                dve.wait_ge(acc_bias, 16 * count)
                sl = lambda i, k_: slice(0, k_) if isinstance(i, int) else bass.ds(i * k_, k_)

                def one_pass(i):
                    lane.after()
                    put(v.tensor_copy(cs_now[:, 0:4], cs[:, sl(i, 4)]))
                    put(v.tensor_copy(cw_now[:, 0:3, :, :], cw4[:, :, :, sl(i, 8)]), cw_ok)
                    put(v.tensor_copy(cw_now[:, 3, :, :], cb3[:, :, sl(i, 8)]), cw_ok)
                    done = 0
                    for pair in range(8):
                        s, r = divmod(pair, 4)
                        q, b = BANK_TURNS[r], r % 2
                        tile = 4 * s + q
                        dve.wait_ge(up_conv.handle, i * 8 + (32 * f + pair + 1))
                        for gv in range(2):
                            for tap in range(2):
                                d = tap + 1
                                u = ps[:, 4 * s + 2 * gv + q // 2, (q % 2) * S:(q % 2 + 1) * S - d]
                                cb = cbuf[:, b, gv, d:S]
                                lane.after()
                                put(v.scalar_tensor_tensor(cb, u, cw_now[:, 1 - tap, gv, tile:tile + 1], cb, ALU.mult, ALU.add),
                                    gconv if (gv == 0 and tap == 1) else None)
                        dve.wait_ge(up_silu.handle, i * 8 + (32 * f + pair + 1))
                        lane.after()
                        dst = act_sb[:, tile, :] if isinstance(i, int) else \
                            wide[:, bass.ds(i * (8 * S) + tile * S, S)]
                        put(v.tensor_tensor(dst, sgate[:, b, :], cbuf[:, b, 1, :], ALU.mult), up_pair)
                        upto = k * (pair + 1) // 8
                        while done < upto:
                            ada_unit(done, thirds, first_ada(n), i * k, cs_now[:, done // len(thirds):done // len(thirds) + 1])
                            done += 1
                one_pass(0)
                with lane.loop(1, 4, {dve_s: 1 + 8 * 3, cw_ok: 2, gconv: 8, up_pair: 8, ada_used: k}, ada_used) as i:
                    one_pass(i)

            ada_group(-1, (0, 1))
            for n in range(4):
                normed(n)
                modulate(n)
                if n == 0:
                    ada_group(0, (2, 0, 1))
                    even_mixer()
                    residual("ev_out", 0, 4)
                elif n == 2:
                    ada_group(2, (2, 0, 1))
                    odd_mixer()
                    residual("od_out", 2, 4)
                else:
                    up(f"up{n // 2}", n // 2)
                    residual(f"down{n // 2}", n, 8)


INPUTS = ["x", "c", "rel_bias", "ada_w", "ada_b", "norm_g", "ev_w_in", "ev_w_out", "nsa_qk_g", "cmp_pe", "cmp_w1", "cmp_b1",
          "cmp_w2", "cmp_b2", "mla_q_norm_g", "mla_kv_norm_g", "mla_w_uq", "mla_w_ukv", "mla_nope_g", "mla_rope_g",
          "od_w_in", "od_w_out", "dsa_qk_g", "ffn_w_up", "ffn_conv_w", "ffn_conv_b", "ffn_w_down"]


def kernel(**inputs):
    import concourse.bacc as bacc
    from concourse.bass_utils import run_bass_kernel_spmd

    nc = bacc.Bacc("TRN2", target_bir_lowering=False, num_devices=1)
    arrays = {n: np.ascontiguousarray(inputs[n]) for n in INPUTS} | constants()
    aps = {n: nc.dram_tensor(f"in_{n}", a.shape, mybir.dt.from_np(a.dtype), kind="ExternalInput").ap() for n, a in arrays.items()}
    out = nc.dram_tensor("out", (1, S, D), F32, kind="ExternalOutput").ap()
    trunk_program(nc, **aps, out=out)
    r = run_bass_kernel_spmd(nc, [{f"in_{n}": a for n, a in arrays.items()}], core_ids=[0])
    return r.results[0]["out"]
```

```python
import math
from contextlib import ExitStack, contextmanager

import numpy as np

import concourse.bass as bass
from concourse import mybir

F32 = mybir.dt.float32
F32R = mybir.dt.float32r
ALU = mybir.AluOpType
ACT = mybir.ActivationFunctionType
AX_X = mybir.AxisListType.X

P = 128
D = 2048
S = 256
ST = S // P
KT = D // P
HD = 128
NSA_H, NSA_G, MLA_H, DSA_H, DSA_KV = 8, 2, 8, 16, 4
Q_RANK, KV_RANK, ROPE = 512, 256, 64
IDX_H, IDX_D, IDX_ROPE = 16, 64, 32
BANK_TURNS = (0, 2, 1, 3)
TOPK = min(256, S // 4)
CMP_BLOCK, CMP_STRIDE, CMP_HID = 32, 16, 256
NCMP = S // CMP_STRIDE - 1
FFN = 4096
FT = FFN // P
BUCKETS, SLOTS, MAX_DIST = 32, 16, 128
EPS, NEG = 1e-6, -1e30
TAKEN = -3e38

E_Q, E_KV, E_GATE = 0, NSA_H * HD, NSA_H * HD + 6 * NSA_G * HD
E_CQ = E_GATE + 3 * NSA_H
E_CKV, E_KPE = E_CQ + Q_RANK, E_CQ + Q_RANK + KV_RANK
E_COLS = E_KPE + ROPE
O_K = DSA_H * HD
O_V = O_K + DSA_KV * HD
O_IQ = O_V + DSA_KV * HD
O_IK = O_IQ + IDX_H * IDX_D
O_IW = O_IK + IDX_D
O_COLS = O_IW + IDX_H

NB = 512
UK = 2
RING = 4
UNIT = UK * NB

ROWS = {}
_at = 0
for _name, _n in (("c", KT), ("norm_g", 4 * KT), ("nsa_g", 2), ("dsa_g", 2), ("nope_g", 2),
                  ("qn_g", Q_RANK // P), ("kvn_g", KV_RANK // P), ("b1", 4)):
    ROWS[_name] = (_at, _n)
    _at += _n
ROWS_A = _at
PE_COL = P
CW_COL = 2 * P
CB_COL = CW_COL + 2 * 3 * 2 * FT
PRM = CB_COL + 2 * 2 * FT

C_ID, C_CAUSAL = 0, P
C_CMASK = C_CAUSAL + S
C_VALID = C_CMASK + ST * NCMP
C_COS64 = C_VALID + ST
C_SIN64 = C_COS64 + ST * ROPE // 2
C_COS32 = C_SIN64 + ST * ROPE // 2
C_SIN32 = C_COS32 + ST * IDX_ROPE // 2
C_FLIP = C_SIN32 + ST * IDX_ROPE // 2
C_COLS = C_FLIP + P
REV = 384
FWD0 = S - 1
FWD = 2 * S


def constants():
    t = np.arange(S)
    con = np.zeros((P, C_COLS), np.float32)
    con[:, C_ID:C_ID + P] = np.eye(P, dtype=np.float32)
    con[:, C_CAUSAL:C_CAUSAL + S] = np.where(t[None, :] <= P + np.arange(P)[:, None], 0.0, NEG)
    ends = np.arange(NCMP) * CMP_STRIDE + CMP_BLOCK - 1
    dist = t[:, None] - ends[None, :]
    con[:, C_CMASK:C_VALID] = np.where(dist >= 0, 0.0, NEG).reshape(ST, P, NCMP).transpose(1, 0, 2).reshape(P, -1)
    con[:, C_VALID:C_COS64] = (dist >= 0).any(1).reshape(ST, P).T

    def rope(dim):
        half = dim // 2
        inv = np.float32(10000.0) ** (-np.arange(half, dtype=np.float32) / np.float32(half))
        ang = t.astype(np.float32)[:, None] * inv[None, :]
        lay = lambda a: a.reshape(ST, P, half).transpose(1, 0, 2).reshape(P, -1)
        return lay(np.cos(ang)), lay(np.sin(ang))

    con[:, C_COS64:C_SIN64], con[:, C_SIN64:C_COS32] = rope(ROPE)
    con[:, C_COS32:C_SIN32], con[:, C_SIN32:C_FLIP] = rope(IDX_ROPE)
    con[:, C_FLIP:C_COLS] = np.eye(P, dtype=np.float32)[::-1]

    def bucket(d):
        n = np.maximum(d, 0)
        exact = BUCKETS // 2
        nf = np.maximum(n, 1).astype(np.float32)
        large = exact + (np.log(nf / np.float32(exact)) / np.float32(math.log(MAX_DIST / exact))
                         * np.float32(BUCKETS - exact)).astype(np.int32)
        return np.where(n < exact, n, np.minimum(large, BUCKETS - 1))

    hot = np.zeros((BUCKETS, REV + FWD), np.float32)
    j = np.arange(REV)
    hot[bucket(S - 1 - j), j] = 1.0
    d = np.arange(FWD) - FWD0
    hot[bucket(d), REV + np.arange(FWD)] = 1.0
    negrow = np.broadcast_to(np.where(j < S, 0.0, NEG).astype(np.float32), (SLOTS, REV))
    return {"k_con": con, "k_hot": hot, "k_neg": np.ascontiguousarray(negrow)}


class Signal:

    def __init__(self, handle):
        self.handle, self.n = handle, 0


class Lane:

    def __init__(self, eng):
        self.eng, self.last = eng, None

    def done(self, ins, sig):
        ins.then_inc(sig.handle, 1)
        sig.n = sig.n + 1
        self.last = (sig, sig.n)

    def after(self):
        if self.last is not None:
            self.eng.wait_ge(self.last[0].handle, self.last[1])

    @contextmanager
    def loop(self, start, end, per, tail):
        base = {s: s.n for s in per}
        assert base[tail] > 0
        self.after()
        with self.eng.Fori(start, end) as i:
            for s, k in per.items():
                s.n = base[s] + (i - start) * k
            self.last = (tail, tail.n)
            yield i
        for s, k in per.items():
            s.n = base[s] + k * (end - start)
        self.last = (tail, tail.n)


NATIVE = "ev_mid"
AHEAD = 3


def weight_plan():
    at, native, plan, skipped = 0, 0, {}, {}
    for name, n in (("ev_in", 56), ("ev_mid", 26), ("ev_out", 32), ("up0", 128), ("down0", 64),
                    ("od_in", 72), ("od_out", 32), ("up1", 128), ("down1", 64)):
        plan[name], skipped[name] = at, native
        at += n
        native += n if name == NATIVE else 0
    return plan, skipped


def even_middle():
    mla = [("mla", b, j) for b in range(3) for j in range(Q_RANK // P // UK)] + [("mla", b, 0) for b in range(3, 7)]
    late = mla[-3:]
    mla, mix = mla[:-3], []
    for j in range(2 * CMP_BLOCK // 4):
        mix.append(("cmp", j // 8, j % 8))
        if (j + 1) * 7 // 16 > j * 7 // 16:
            mix.append(mla.pop(0))
    return mix, late


def trunk_program(nc, x, c, rel_bias, ada_w, ada_b, norm_g, ev_w_in, ev_w_out, nsa_qk_g, cmp_pe, cmp_w1, cmp_b1,
                  cmp_w2, cmp_b2, mla_q_norm_g, mla_kv_norm_g, mla_w_uq, mla_w_ukv, mla_nope_g, mla_rope_g,
                  od_w_in, od_w_out, dsa_qk_g, ffn_w_up, ffn_conv_w, ffn_conv_b, ffn_w_down,
                  k_con, k_hot, k_neg, out):
    PLAN, SKIPPED = weight_plan()
    MIX, MIX_LATE = even_middle()
    assert len(MIX + MIX_LATE) == PLAN["ev_out"] - PLAN["ev_mid"]

    def mix_end(*unit):
        return PLAN["ev_mid"] + (MIX + MIX_LATE).index(unit) + 1

    def nth(name, u, k):
        return UK * (PLAN[name] + u - SKIPPED[name]) + k + 1

    PAIRS_BEFORE = {(0, "in"): 0, (0, "out"): 8, (1, "in"): 16, (1, "out"): 24,
                    (2, "in"): 40, (2, "out"): 48, (3, "in"): 56, (3, "out"): 64}
    ctx = ExitStack()
    with ctx:
        def sb(name, shape, dt=F32):
            return ctx.enter_context(nc.sbuf_tensor(name, shape, dt))

        def sem(name):
            return ctx.enter_context(nc.semaphore(name))

        def sig(name):
            return Signal(sem(name))

        x_sb = sb("x_sb", [P, ST, D])
        with nc.sbuf_tensor("hT", [P, KT, S], F32) as hT:
            pass
        hT_lo = sb("hT_lo", [P, KT, S], F32R)
        bias = sb("bias", [P, SLOTS, S])
        acc = sb("acc", [P, 3, D])
        aring = sb("aring", [P, 2, D])
        ring_hi = sb("ring_hi", [P, RING, UNIT], F32R)
        with nc.sbuf_tensor("ring", [P, RING, UNIT], F32) as ring:
            pass
        ring_lo = sb("ring_lo", [P, RING, UNIT], F32R)
        con = sb("con", [P, C_COLS])
        prm = sb("prm", [P, PRM])
        ropeg = sb("ropeg", [P, 2 * ROPE])
        ones = sb("ones", [P, P])
        cs = sb("cs", [P, KT])
        cs_now = sb("cs_now", [P, 6])
        cw_now = sb("cw_now", [P, 2, 4, 2, 4])
        modc = sb("modc", [P, 2, KT])
        xst = sb("xst", [P, 4, ST])
        st = sb("st", [P, 64])
        nmx = sb("nmx", [P, 3, 2])
        sm = sb("sm", [P, 3, 2])
        rw = sb("rw", [P, 3, 2])
        cbias = sb("cbias", [P, ST, NCMP, NSA_H])
        gs = sb("gs", [P, 3])

        NORMED = ST * O_COLS
        SPLIT = NORMED + ST * D

        def layout(*tensors):
            with ExitStack() as region:
                return [region.enter_context(nc.sbuf_tensor(*t)) for t in tensors]

        wide, side, kT, kpT, qT, knT, qpT, L, PT = layout(
            ("wide", [P, NORMED], F32),
            ("side", [P, 7168], F32),
            ("kT", [P, 4, S], F32), ("kpT", [ROPE, S], F32), ("qT", [P, 2, S], F32), ("knT", [P, 2, S], F32),
            ("qpT", [ROPE, 2, S], F32),
            ("L", [P, 3, 3 * P], F32),
            ("PT", [P, 2, 3 * P], F32))
        _, first_ring = layout(("below_first_ring", [P, NORMED + 7168], F32), ("first_ring", [P, 2, D], F32))
        _, hT_hi = layout(("below_hT_hi", [P, SPLIT], F32), ("hT_hi", [P, KT, S], F32R))
        actF, = layout(("actF", [P, FT * S], F32))
        act_lo, _, act_hi = layout(("act_lo", [P, FT, S], F32R), ("below_act_hi", [P, NORMED - FT * S], F32),
                                   ("act_hi", [P, FT, S], F32R))
        _, cbuf, sgate, rtmp = layout(("below_cbuf", [P, SPLIT + KT * S], F32),
                                      ("cbuf", [P, 2, 2, S], F32),
                                      ("sgate", [P, 2, S], F32),
                                      ("rtmp", [P, 2, NB], F32))
        ps = ctx.enter_context(nc.psum_tensor("ps", [P, 8, 512], F32))
        toeplitz = nc.dram_tensor("toeplitz", (SLOTS, REV), F32, kind="Internal").ap()

        ident = con[:, C_ID:C_ID + P]
        causal = con[:, C_CAUSAL:C_CAUSAL + S]
        valid = con[:, C_VALID:C_VALID + ST]
        ev = wide[:, 0:ST * E_COLS].rearrange("p (t n) -> p t n", t=ST)
        od = wide[:, 0:ST * O_COLS].rearrange("p (t n) -> p t n", t=ST)
        xn = side[:, 0:ST * D].rearrange("p (t n) -> p t n", t=ST)
        KVF = MLA_H * 2 * HD
        QF = MLA_H * (HD + ROPE)
        kvf = side[:, 0:ST * KVF].rearrange("p (t n) -> p t n", t=ST)
        qf = side[:, ST * KVF:ST * (KVF + QF)].rearrange("p (t n) -> p t n", t=ST)
        flat = side[:, 0:2 * CMP_BLOCK * 30].rearrange("p (a l r) -> p a l r", a=2, l=CMP_BLOCK)
        rows = side[:, 4096:4096 + 6 * P].rearrange("p (r n) -> p r n", r=6)
        rev = side[0:SLOTS, 5120:5120 + REV]
        negrow = side[0:SLOTS, 5632:5632 + REV]
        hot = side[0:BUCKETS, 6016:6016 + REV + FWD]
        tbl = side[0:BUCKETS, 6912:6912 + SLOTS]
        tail = ST * E_COLS
        w2 = wide[:, tail:tail + 512].rearrange("p (a k n) -> p a k n", a=2, k=2)
        b2 = wide[0:1, tail + 512:tail + 768]
        kc = wide[0:NCMP, tail + 768:tail + 1024]
        vc = wide[0:NCMP, tail + 1024:tail + 1280]
        hid = wide[:, tail + 1280:tail + 1400].rearrange("p (a k r) -> p a k r", a=2, k=2)
        kcT = wide[:, tail + 1400:tail + 1400 + NSA_G * NCMP]
        hotr, hotf = hot[:, 0:REV], hot[:, REV:REV + FWD]
        iqT = side[:, 0:512].rearrange("p (b s) -> p b s", b=2)
        ikT = side[:, 512:768]
        ikd = side[:, 768:1024].rearrange("p (t n) -> p t n", t=ST)
        rel = side[:, 1024:1024 + 768].rearrange("p (b s) -> p b s", b=2)
        isc = side[:, 1792:1792 + 384]
        iwk = side[:, 2176:2176 + 384]
        _, selm, ident_r = layout(("below_selm", [P, NORMED + 2560], F32), ("selm", [P, 3 * P], F32R),
                                  ("ident_r", [P, P], F32R))
        m8 = side[:, 3072:3088].rearrange("p (t n) -> p t n", t=ST)
        scr = side[:, 3072:7168]

        msq = PT[:, :, :].rearrange("p b (k n) -> p (b k) n", k=3)

        def act_pair(u):
            return actF[:, 2 * u * S:(2 * u + 2) * S].rearrange("p (f s) -> p f s", f=2)

        def turns_for(u):
            return 4 * (u // 2) + 3 + u % 2

        squared = cbuf[:, :, :, :].rearrange("p b g (k n) -> p (b g k) n", k=2)

        mean_q, mean_k = (st[:, 0:48].rearrange("p (t n) -> p t n", t=ST)[:, :, c0:c1] for c0, c1 in ((0, 16), (16, 24)))

        params_in = sem("params_in")
        x_in = sem("x_in")
        rows_in = sem("rows_in")
        landed = [sem(f"landed{s}") for s in range(RING)]
        ada_landed = [sem(f"ada_landed{s}") for s in range(4)]
        toep_out, toep_in, out_stored = sem("toep_out"), sem("toep_in"), sem("out_stored")
        acc_bias = sem("acc_bias")
        unit_used = sig("unit_used")
        dve_s = sig("dve_s")
        ada_used = sig("ada_used")
        acc_clear = sig("acc_clear")
        cols_done = sig("cols_done")
        hi_ok, lo_ok = sig("hi_ok"), sig("lo_ok")
        h_hi, h_lo = sig("h_hi"), sig("h_lo")
        prm_T = sig("prm_T")
        prm_ok = sig("prm_ok")
        cs_ok, ones_ok = sig("cs_ok"), sig("ones_ok")
        modc_ok = sig("modc_ok")
        xsq, xsd, xn_ok = sig("xsq"), sig("xsd"), sig("xn_ok")
        xT = sig("xT")
        hT_act, hT_dve = sig("hT_act"), sig("hT_dve")
        proj_out = sig("proj_out")
        gate_red, gate_ok = sig("gate_red"), sig("gate_ok")
        res_out = sig("res_out")
        up_conv, up_silu, up_pair = sig("up_conv"), sig("up_silu"), sig("up_pair")
        cw_ok, gconv = sig("cw_ok"), sig("gconv")
        rev_mm, rev_ok, cb_mm, cb_ok = sig("rev_mm"), sig("rev_ok"), sig("cb_mm"), sig("cb_ok")

        (ev_sq, ev_var, ev_nrm, gates_raw, gates_ok, ek_T, ek_ok, flat_ok, hid_ok, kc_T, kc_sq, kc_var, kc_ok, kcT_ok,
         vc_ok, mla_out, mla_sq, mla_var, mla_nrm) = (sig(n) for n in (
             "ev_sq", "ev_var", "ev_nrm", "gates_raw", "gates_ok", "ek_T", "ek_ok", "flat_ok", "hid_ok", "kc_T", "kc_sq",
             "kc_var", "kc_ok", "kcT_ok", "vc_ok", "mla_out", "mla_sq", "mla_var", "mla_nrm"))
        (od_sq, od_var, od_nrm, dk_T, dk_ok, irope, iq_T, iq_ok, idx_mm, irel, isum) = (sig(n) for n in (
            "od_sq", "od_var", "od_nrm", "dk_T", "dk_ok", "irope", "iq_T", "iq_ok", "idx_mm", "irel", "isum"))

        sel_ok, ident_ok = sig("sel_ok"), sig("ident_ok")
        flipped, bias_ok = sig("flipped"), sig("bias_ok")

        block = ctx.enter_context(nc.Block())

        def wsrc(w, k0, kn, c0, n):
            return w[k0 * P:(k0 + kn) * P, c0:c0 + n] if isinstance(c0, int) else w[k0 * P:(k0 + kn) * P, bass.ds(c0, n)]

        n_params = [0]

        @block.sync
        def _(sp):
            def row_load(r, at, src):
                n = src.shape[0]
                sp.dma_start(rows[at:at + n, r, :], src).then_inc(rows_in, 16)
                n_params[0] += 1

            row_load(0, ROWS["c"][0], c.rearrange("o (k p) -> (o k) p", p=P))
            row_load(0, ROWS["norm_g"][0], norm_g.rearrange("i j (k p) -> (i j k) p", p=P))
            row_load(0, ROWS["nsa_g"][0], nsa_qk_g.rearrange("o g p -> (o g) p"))
            row_load(0, ROWS["dsa_g"][0], dsa_qk_g.rearrange("o g p -> (o g) p"))
            row_load(0, ROWS["nope_g"][0], mla_nope_g.rearrange("o g p -> (o g) p"))
            row_load(0, ROWS["qn_g"][0], mla_q_norm_g.rearrange("o (k p) -> (o k) p", p=P))
            row_load(0, ROWS["kvn_g"][0], mla_kv_norm_g.rearrange("o (k p) -> (o k) p", p=P))
            row_load(0, ROWS["b1"][0], cmp_b1.rearrange("o g (k p) -> (o g k) p", p=P))
            row_load(1, 0, cmp_pe.rearrange("o g l p -> (o g l) p"))
            cw = ffn_conv_w.rearrange("l j (k p) -> (l j k) p", p=P)
            for r in range(3):
                row_load(2 + r, 0, cw[r * P:(r + 1) * P, :])
            row_load(5, 0, ffn_conv_b.rearrange("l (k p) -> (l k) p", p=P))
            for dst, src in ((con[:, :], k_con), (hot, k_hot), (negrow, k_neg), (tbl, rel_bias),
                             (w2, cmp_w2.rearrange("o g (k p) n -> p (o g) k n", p=P)),
                             (b2, cmp_b2.rearrange("o g n -> o (g n)")),
                             (ropeg[:, :], bass.AP(mla_rope_g.tensor, 0, [[0, P], [1, 2 * ROPE]]))):
                sp.dma_start(dst, src).then_inc(params_in, 16)
            sp.dma_start(x_sb[:, :, :], x.rearrange("o (t p) n -> p (o t) n", p=P)).then_inc(x_in, 16)

            def unit(idx, u, src, dst):
                if not (isinstance(idx, int) and idx < RING):
                    sp.wait_ge(unit_used.handle, idx - (RING - 1))
                sp.dma_start(dst, src).then_inc(landed[u % RING], 16)

            def matrix(first, w, units, c0, n, idx_extra=0):
                for u in range(units):
                    g = first + u
                    src = wsrc(w, u * UK, UK, c0, n).rearrange("(k p) n -> p k n", p=P)
                    dst = ring[:, g % RING, 0:UK * n].rearrange("p (k n) -> p k n", k=UK)
                    unit(g + idx_extra, g, src, dst)

            matrix(0, ev_w_in[0], 8, 0, NB)
            matrix(8, ev_w_in[0], 8, NB, NB)
            with sp.Fori(1, 3) as i:
                for b in range(2):
                    matrix(8 * b, ev_w_in[0], 8, i * (2 * NB) + b * NB, NB, i * 16)
            matrix(48, ev_w_in[0], 8, 6 * NB, E_COLS - 6 * NB)
            for m, (kind, a, u) in enumerate(MIX + MIX_LATE):
                g = PLAN["ev_mid"] + m
                if kind == "cmp":
                    w1 = cmp_w1[0, a].rearrange("(l p) n -> p l n", p=P)
                    unit(g, g, w1[:, 4 * u:4 * u + 4, :], ring[:, g % RING, :].rearrange("p (l n) -> p l n", l=4))
                elif a < 3:
                    matrix(g, mla_w_uq[0][u * UK * P:(u + 1) * UK * P, :], 1, a * NB, NB)
                else:
                    matrix(g, mla_w_ukv[0], 1, (a - 3) * NB, NB)

            def narrow(name, w, units):
                with sp.Fori(0, 2) as i:
                    for b in range(2):
                        matrix(PLAN[name] + units * b, w, units, i * (2 * NB) + b * NB, NB, i * (2 * units))

            def up(name, w):
                with sp.Fori(0, 4) as i:
                    for s in range(2):
                        for gv in range(2):
                            matrix(PLAN[name] + 16 * s + 8 * gv, w, 8, i * (2 * NB) + (s * NB + gv * FFN), NB, i * 32)

            narrow("ev_out", ev_w_out[0], 8)
            up("up0", ffn_w_up[0])
            narrow("down0", ffn_w_down[0], 16)
            with sp.Fori(0, 4) as i:
                for b in range(2):
                    matrix(PLAN["od_in"] + 8 * b, od_w_in[0], 8, i * (2 * NB) + b * NB, NB, i * 16)
            matrix(PLAN["od_in"] + 64, od_w_in[0], 8, 8 * NB, O_COLS - 8 * NB)
            narrow("od_out", od_w_out[0], 8)
            up("up1", ffn_w_up[1])
            narrow("down1", ffn_w_down[1], 16)
            for b in range(4):
                sp.wait_ge(res_out.handle, 3 * 4 + b + 1)
                sp.dma_start(out.rearrange("o (t p) n -> p (o t) n", p=P)[:, :, b * NB:(b + 1) * NB],
                             x_sb[:, :, b * NB:(b + 1) * NB]).then_inc(out_stored, 16)
            sp.wait_ge(out_stored, 64)

        FIRST_MOD = 2 * KT
        MOD_PASSES = (3, 4, 4, 4)
        ONE, TWO = [(0, 1, 0), (1, 1, 0)], [(0, 2, 0), (1, 2, 0), (0, 2, 1), (1, 2, 1)]
        GATE4 = [(2, 4, k) for k in range(4)]
        MOD_PASS = (GATE4 + ONE, GATE4 + TWO, GATE4 + ONE, GATE4)
        MOD_REST = ([(2, k) for k in range(12, KT)] + [(t, k) for k in range(3, KT) for t in (0, 1)],
                    [(t, k) for k in range(8, KT) for t in (0, 1)],
                    [(t, k) for k in range(4, KT) for t in (0, 1)], [])
        GATE_UNITS = (3 * 6 + 4, 4 * 8, 4 * 6, KT)

        def first_mod(n):
            return FIRST_MOD + 3 * KT * n

        def mod_slot(m):
            if m < FIRST_MOD:
                return (aring[:, m % 4, :] if m % 4 < 2 else first_ring[:, m % 4 - 2, :]), ada_landed[m % 4], m // 4
            return aring[:, m % 2, :], ada_landed[m % 2], FIRST_MOD // 4 + (m - FIRST_MOD) // 2

        CLEARED = (2, 5, 8, 11, 12)

        @block.gpsimd
        def _(pool):
            lane = Lane(pool)
            lane.done(nc.gpsimd.memset(ones[:, :], 1.0), ones_ok)

            def clear(n, thirds):
                for t in thirds:
                    lane.done(nc.gpsimd.memset(acc[:, t, :], 0.0), acc_clear)
                lane.after()
                for t in thirds:
                    m = n if t == 2 else n + 1
                    pool.dma_start(acc[0:1, t, :], ada_b[m // 2, m % 2:m % 2 + 1, t * D:(t + 1) * D]).then_inc(acc_bias, 16)

            def load(m, n, t, k, extra=0):
                slot, landed_, _ = mod_slot(m)
                slots = 4 if m < FIRST_MOD else 2
                if not (isinstance(extra, int) and m < slots):
                    pool.wait_ge(ada_used.handle, extra + (m - slots + 1))
                l = n if t == 2 else n + 1
                w = ada_w[l // 2, l % 2]
                src = w[k * P:(k + 1) * P, t * D:(t + 1) * D] if isinstance(k, int) else w[bass.ds(k * P, P), t * D:(t + 1) * D]
                pool.dma_start(slot, src).then_inc(landed_, 16)

            clear(-1, (0, 1))

            def first_pass(i):
                for j in range(4):
                    load(j, -1, j % 2, i * 2 + j // 2, i * 4)
            first_pass(0)
            with pool.Fori(1, KT // 2) as i:
                first_pass(i)
            for n in range(4):
                if n < 3:
                    pool.wait_ge(cols_done.handle, n + 1)
                if n > 0:
                    pool.wait_ge(res_out.handle, 4 * n)
                clear(n, (2, 0, 1) if n < 3 else (2,))
                per = len(MOD_PASS[n])
                with pool.Fori(0, MOD_PASSES[n]) as i:
                    for j, (t, step, k) in enumerate(MOD_PASS[n]):
                        load(first_mod(n) + j, n, t, i * step + k, i * per)
                for j, (t, k) in enumerate(MOD_REST[n]):
                    load(first_mod(n) + per * MOD_PASSES[n] + j, n, t, k)

        EV_UNITS = []
        for h in range(NSA_H):
            EV_UNITS += [("cmp", h), ("slc", h), ("win", h)]
        EV_UNITS += [("mla", h) for h in range(MLA_H)]
        OD_UNITS = [("dsa", h) for h in range(DSA_H)]

        def qheads(units):
            n, res, last = -1, [], None
            for kind, h in units:
                key = (kind == "mla", h)
                if key != last:
                    n, last = n + 1, key
                res.append(n)
            return res

        class Att:

            def __init__(self, tag, units):
                self.units, self.qh = units, qheads(units)
                self.q_raw, self.q_ok = sig(f"{tag}_q_raw"), sig(f"{tag}_q_ok")
                self.s_ok = sig(f"{tag}_s_ok")
                self.l_ok = sig(f"{tag}_l_ok")
                self.p_ok = sig(f"{tag}_p_ok")
                self.w_ok = sig(f"{tag}_w_ok")
                self.scaled = sig(f"{tag}_scaled")
                self.t_ok, self.pt_ok = sig(f"{tag}_t_ok"), sig(f"{tag}_pt_ok")
                self.o_ok, self.o_out = sig(f"{tag}_o_ok"), sig(f"{tag}_o_out")
                self.last_of = [n for n in range(len(units)) if n + 1 == len(units) or self.qh[n + 1] != self.qh[n]]
                self.first_of = [0] + [n + 1 for n in self.last_of[:-1]]

        EVA, ODA = Att("ev", EV_UNITS), Att("od", OD_UNITS)
        LAG = 2
        S_B, T_B, O_B, Q_B = 0, 2, 4, 6

        def q_cols(att, n):
            kind, h = att.units[n]
            if kind == "dsa":
                return [od[:, t, h * HD:(h + 1) * HD] for t in range(ST)]
            if kind == "mla":
                return [qf[:, t, h * (HD + ROPE):h * (HD + ROPE) + HD] for t in range(ST)]
            return [ev[:, t, E_Q + h * HD:E_Q + (h + 1) * HD] for t in range(ST)]

        def kv_col(which, g):
            return E_KV + (which * NSA_G + g) * HD

        def pe_attention(pe, lane, att):
            units, qh = att.units, att.qh

            def queries(n):
                if n >= len(units) or n not in att.first_of:
                    return
                q = qh[n]
                b = q % 2
                kind, h = units[n]
                if q >= (1 if kind == "mla" else 2):
                    pe.wait_ge(att.q_ok.handle, q if kind == "mla" else q - 1)
                if kind == "mla":
                    for t in range(ST):
                        nc.tensor.transpose(ps[0:ROPE, Q_B + 1, t * P:(t + 1) * P],
                                            qf[:, t, h * (HD + ROPE) + HD:(h + 1) * (HD + ROPE)], ident)
                    for t in range(ST):
                        nc.tensor.transpose(ps[:, Q_B, S + t * P:S + (t + 1) * P], kvf[:, t, h * 2 * HD:h * 2 * HD + HD], ident)
                    b = 0
                for t, col in enumerate(q_cols(att, n)):
                    ins = nc.tensor.transpose(ps[:, Q_B + b, t * P:(t + 1) * P], col, ident)
                lane.done(ins, att.q_raw)

            def logits(n):
                q, b = qh[n], S_B + n % 2
                kind, h = units[n]
                pe.wait_ge(att.q_ok.handle, q + 1)
                if n >= 2:
                    pe.wait_ge(att.l_ok.handle, n - 1)
                qs = qT[:, q % 2, :]
                if kind == "cmp":
                    g = h // (NSA_H // NSA_G)
                    for t in range(ST):
                        ins = nc.tensor.matmul(ps[:, b, t * P:t * P + NCMP], qs[:, t * P:(t + 1) * P],
                                               kcT[:, g * NCMP:(g + 1) * NCMP], start=True, stop=True)
                else:
                    for t, off, nk in ((1, 0, S), (0, S, P)):
                        parts = []
                        if kind == "mla":
                            parts = [(qs[:, t * P:(t + 1) * P], knT[:, q % 2, 0:nk]),
                                     (qpT[:, q % 2, t * P:(t + 1) * P], kpT[:, 0:nk])]
                        else:
                            k = {"slc": h // 4, "win": 2 + h // 4, "dsa": h // 4}[kind]
                            parts = [(qs[:, t * P:(t + 1) * P], kT[:, k, 0:nk])]
                            if kind == "dsa":
                                parts.append((ident_r[:, :], selm[:, off:off + nk]))
                        for j, (l, r) in enumerate(parts):
                            ins = nc.tensor.matmul(ps[:, b, off:off + nk], l, r, start=j == 0, stop=j == len(parts) - 1)
                lane.done(ins, att.s_ok)

            def output(n):
                kind, h = units[n]
                b = T_B + n % 2
                pe.wait_ge(att.scaled.handle, n + 1)
                if n >= 2:
                    pe.wait_ge(att.pt_ok.handle, n - 1)
                p = L[:, n % 3, :]
                if kind == "cmp":
                    for t in range(ST):
                        ins = nc.tensor.transpose(ps[0:NCMP, b, t * P:(t + 1) * P], p[:, t * NCMP:(t + 1) * NCMP], ident)
                else:
                    nc.tensor.transpose(ps[:, b, 0:P], p[:, S:S + P], ident)
                    nc.tensor.transpose(ps[:, b, P:2 * P], p[:, 0:P], ident)
                    ins = nc.tensor.transpose(ps[:, b, 2 * P:3 * P], p[:, P:2 * P], ident)
                lane.done(ins, att.t_ok)

            def values(n):
                kind, h = units[n]
                q = qh[n]
                first, last = n in att.first_of, n in att.last_of
                if first and q >= 2:
                    pe.wait_ge(att.o_out.handle, q - 1)
                pe.wait_ge(att.pt_ok.handle, n + 1)
                o = ps[:, O_B + q % 2, 0:S]
                g = h // 4
                if kind == "cmp":
                    ins = nc.tensor.matmul(o, vc[:, g * HD:(g + 1) * HD], PT[0:NCMP, n % 2, 0:S], start=first, stop=last)
                else:
                    v = {"slc": lambda t: ev[:, t, kv_col(3, g):kv_col(3, g) + HD],
                         "win": lambda t: ev[:, t, kv_col(5, g):kv_col(5, g) + HD],
                         "mla": lambda t: kvf[:, t, h * 2 * HD + HD:(h + 1) * 2 * HD],
                         "dsa": lambda t: od[:, t, O_V + g * HD:O_V + (g + 1) * HD]}[kind]
                    late = ps[:, O_B + q % 2, P:S]
                    if first:
                        nc.tensor.matmul(late, v(1), PT[:, n % 2, 2 * P:3 * P], start=True, stop=False)
                        nc.tensor.matmul(late, v(0), PT[:, n % 2, P:S], start=False, stop=True)
                        ins = nc.tensor.matmul(ps[:, O_B + q % 2, 0:P], v(0), PT[:, n % 2, 0:P], start=True, stop=True)
                    else:
                        nc.tensor.matmul(late, v(1), PT[:, n % 2, 2 * P:3 * P], start=False, stop=False)
                        ins = nc.tensor.matmul(o, v(0), PT[:, n % 2, 0:S], start=False, stop=last)
                lane.done(ins, att.o_ok)

            queries(0)
            for n in range(len(units) + LAG + 1):
                queries(n + 1)
                if n < len(units):
                    logits(n)
                if 0 <= n - LAG < len(units):
                    output(n - LAG)
                if 0 <= n - LAG - 1 < len(units):
                    values(n - LAG - 1)

        @block.tensor
        def _(pe):
            lane = Lane(pe)

            def wait_unit(u, extra=0):
                pe.wait_ge(landed[u % RING], extra * 4 + 16 * (u // RING + 1))

            pe.wait_ge(rows_in, 16 * n_params[0])
            pe.wait_ge(params_in, 16 * 7)
            for r, (n, at) in enumerate(((ROWS_A, 0), (2 * CMP_BLOCK, PE_COL), (P, CW_COL), (P, CW_COL + P),
                                         (P, CW_COL + 2 * P), (P, CB_COL))):
                ins = nc.tensor.transpose(ps[:, r // 4, (r % 4) * P:(r % 4) * P + n], rows[0:n, r, :], con[0:n, C_ID:C_ID + n])
            lane.done(ins, prm_T)
            ins = nc.tensor.matmul(ps[0:SLOTS, 2, 0:REV], tbl[:, :], hotr, start=True, stop=True)
            lane.done(ins, rev_mm)
            for t in range(ST):
                for j in range(NCMP):
                    d0 = FWD0 + t * P - CMP_STRIDE * j - (CMP_BLOCK - 1)
                    ins = nc.tensor.matmul(ps[:, 3, (t * NCMP + j) * NSA_H:(t * NCMP + j + 1) * NSA_H],
                                           hotf[:, d0:d0 + P], tbl[:, 0:NSA_H], start=True, stop=True)
            lane.done(ins, cb_mm)

            pe.wait_ge(toep_in, 16)
            pe.wait_ge(prm_ok.handle, 4)
            pe.wait_ge(cb_ok.handle, 1)
            for b in range(8):
                ins = nc.tensor.matmul(ps[:, b, :], con[:, C_FLIP:C_FLIP + P], wide[:, b * 512:(b + 1) * 512], start=True, stop=True)
            lane.done(ins, flipped)
            pe.wait_ge(bias_ok.handle, 8)

            def modulation(n):
                pe.wait_ge(ones_ok.handle, 1)
                for t in range(2):
                    pe.wait_ge(ada_used.handle, first_mod(n) - 1 + t)
                    for j in range(KT):
                        ins = nc.tensor.matmul(ps[:, 7, t * KT + j:t * KT + j + 1], acc[:, t, j * P:(j + 1) * P], ones[:, 0:1],
                                               start=True, stop=True)
                lane.done(ins, cols_done)

            def normed(n, banks):
                pe.wait_ge(xn_ok.handle, 2 * (n + 1))
                for b in banks:
                    if b == 3:
                        pe.wait_ge(modc_ok.handle, 2 * (n + 1))
                    if b >= 4:
                        pe.wait_ge((hT_act if b % 2 == 0 else hT_dve).handle, 8 * n + 2 * ((b - 4) // 2 + 1))
                    for k in range(2):
                        for t in range(ST):
                            ins = nc.tensor.transpose(ps[:, 4 + b % 4, k * S + t * P:k * S + (t + 1) * P],
                                                      xn[:, t, (2 * b + k) * P:(2 * b + k + 1) * P], ident)
                    lane.done(ins, xT)

            h_parts = ((lambda k: hT_hi[:, k, :]), (lambda k: hT_lo[:, k, :]))
            act_parts = ((lambda k: act_hi[:, k, :]), (lambda k: act_lo[:, k, :]))

            def rows_block(name, first, units, n, bank, left, extra=0, pairs_before=None):
                for u in range(units):
                    g = PLAN[name] + first + u
                    if pairs_before is not None:
                        pe.wait_ge(h_lo.handle, pairs_before + u + 1)
                    w_hi, w_lo = (r[:, g % RING, 0:UK * n].rearrange("p (k n) -> p k n", k=UK)
                                  for r in (ring_hi, ring_lo))
                    for k in range(UK):
                        start, stop = u == 0 and k == 0, u == units - 1 and k == UK - 1
                        pe.wait_ge(lo_ok.handle, extra * UK + nth(name, first + u, k))
                        for t in range(ST):
                            o, rows_ = ps[:, bank + t, 0:n], slice(t * P, (t + 1) * P)
                            hi, lo = (part(u * UK + k)[:, rows_] for part in left)
                            nc.tensor.matmul(o, hi, w_hi[:, k, :], start=start, stop=False)
                            nc.tensor.matmul(o, hi, w_lo[:, k, :], start=False, stop=False)
                            ins = nc.tensor.matmul(o, lo, w_hi[:, k, :], start=False, stop=stop)
                    lane.done(ins, unit_used)

            def in_proj(name, n, pairs, cols, seen):
                rows_block(name, 0, 8, NB, 0, h_parts, pairs_before=PAIRS_BEFORE[n, "in"])
                rows_block(name, 8, 8, NB, 2, h_parts)
                base = unit_used.n
                with pe.Fori(1, pairs) as i:
                    for b in range(2):
                        pe.wait_ge(proj_out.handle, i * 2 + (seen + b - 1))
                        rows_block(name, 8 * b, 8, NB, 2 * b, h_parts, i * 16)
                unit_used.n = base + (pairs - 1) * 16
                pe.wait_ge(proj_out.handle, seen + 2 * pairs - 1)
                rows_block(name, 16 * pairs, 8, cols - 2 * pairs * NB, 0, h_parts)

            def gate_rows(n):
                pe.wait_ge(ada_used.handle, first_mod(n) + GATE_UNITS[n])
                for j in range(4):
                    ins = nc.tensor.matmul(ps[:, 4 + j, :], ones[:, :], acc[:, 2, j * NB:(j + 1) * NB], start=True, stop=True)
                lane.done(ins, gate_red)

            def out_side(name, n, units, left):
                rows_block(name, 0, units, NB, 0, left, pairs_before=PAIRS_BEFORE[n, "out"])
                if n % 2 == 1:
                    pe.wait_ge(up_pair.handle, 32 * (n // 2 + 1))
                gate_rows(n)
                rows_block(name, units, units, NB, 2, left)
                for b in range(2):
                    pe.wait_ge(res_out.handle, 4 * n + 1 + b)
                    rows_block(name, units * (2 + b), units, NB, 2 * b, left)

            def up(name, f):
                def one_pass(i):
                    for s in range(2):
                        if f > 0 or not isinstance(i, int):
                            pe.wait_ge(up_pair.handle, i * 8 + (32 * f + 4 * s - 4))
                        for gv in range(2):
                            for u in range(8):
                                at = 16 * s + 8 * gv + u
                                g = PLAN[name] + at
                                if isinstance(i, int) and at < 8:
                                    pe.wait_ge(h_lo.handle, PAIRS_BEFORE[2 * f + 1, "in"] + u + 1)
                                w_hi, w_lo = (r[:, g % RING, :].rearrange("p (k n) -> p k n", k=UK) for r in (ring_hi, ring_lo))
                                for k in range(UK):
                                    pe.wait_ge(lo_ok.handle, i * (32 * UK) + nth(name, at, k))
                                    for q in range(4):
                                        o = ps[:, 4 * s + 2 * gv + q // 2, (q % 2) * S:(q % 2 + 1) * S]
                                        hi, lo = (w[:, k, q * P:(q + 1) * P] for w in (w_hi, w_lo))
                                        start, stop = u == 0 and k == 0 and q % 2 == 0, u == 7 and k == UK - 1
                                        kt = u * UK + k
                                        nc.tensor.matmul(o, hi, hT_hi[:, kt, :], start=start, stop=False, skip_group_check=True)
                                        nc.tensor.matmul(o, hi, hT_lo[:, kt, :], start=False, stop=False, skip_group_check=True)
                                        ins = nc.tensor.matmul(o, lo, hT_hi[:, kt, :], start=False, stop=stop,
                                                               skip_group_check=True)
                                lane.done(ins, unit_used)
                one_pass(0)
                with lane.loop(1, 4, {unit_used: 32}, unit_used) as i:
                    one_pass(i)

            def even_mixer():
                for a in range(2):
                    for g in range(NSA_G):
                        for t in range(ST):
                            ins = nc.tensor.transpose(ps[:, 6 + a, g * S + t * P:g * S + (t + 1) * P],
                                                      ev[:, t, kv_col(a, g):kv_col(a, g) + HD], ident)
                lane.done(ins, ek_T)
                pe.wait_ge(ev_nrm.handle, 12)
                for j, (which, g) in enumerate(((2, 0), (2, 1), (4, 0), (4, 1))):
                    for t in range(ST):
                        ins = nc.tensor.transpose(ps[:, 4 + j // 2, (j % 2) * S + t * P:(j % 2) * S + (t + 1) * P],
                                                  ev[:, t, kv_col(which, g):kv_col(which, g) + HD], ident)
                lane.done(ins, ek_T)
                for b in range(3):
                    if b < 2:
                        pe.wait_ge(ek_ok.handle, b + 1)
                    else:
                        pe.wait_ge(flat_ok.handle, 4)
                    for k in range(2):
                        col = (E_CQ + (2 * b + k) * P) if b < 2 else E_CKV + k * P
                        for t in range(ST):
                            ins = nc.tensor.transpose(ps[:, 4 + b, k * S + t * P:k * S + (t + 1) * P], ev[:, t, col:col + P], ident)
                    lane.done(ins, ek_T)
                pe.wait_ge(flat_ok.handle, 8)
                for t in range(ST):
                    ins = nc.tensor.transpose(ps[0:ROPE, 7, t * P:(t + 1) * P], ev[:, t, E_KPE:E_KPE + ROPE], ident)
                lane.done(ins, ek_T)
                pe.wait_ge(ek_ok.handle, 9)

                def mix(units):
                    for kind, a, u in units:
                        g = mix_end(kind, a, u) - 1
                        if kind == "mla" and a >= 2 and u == 0:
                            pe.wait_ge(mla_out.handle, a - 1)
                        wait_unit(g)
                        if kind == "cmp":
                            w = ring[:, g % RING, :].rearrange("p (l n) -> p l n", l=4)
                            for l in range(4):
                                for hc in range(2):
                                    ins = nc.tensor.matmul(ps[:, 4 + 2 * a + hc, 0:NSA_G * NCMP], w[:, l, hc * P:(hc + 1) * P],
                                                           flat[:, a, 4 * u + l, :], start=(u == 0 and l == 0), stop=(u == 7 and l == 3))
                        else:
                            w = ring[:, g % RING, :].rearrange("p (k n) -> p k n", k=UK)
                            first, tiles = (8, Q_RANK // P) if a < 3 else (12, KV_RANK // P)
                            for k in range(UK):
                                kt = u * UK + k
                                for t in range(ST):
                                    ins = nc.tensor.matmul(ps[:, 2 * (a % 2) + t, :], hT[:, first + kt, t * P:(t + 1) * P], w[:, k, :],
                                                           start=kt == 0, stop=kt == tiles - 1)
                        lane.done(ins, unit_used)

                mix(MIX)
                pe.wait_ge(hid_ok.handle, 4)
                for a in range(2):
                    for g in range(NSA_G):
                        o = ps[0:NCMP, 4 + a, g * HD:(g + 1) * HD]
                        for hc in range(2):
                            nc.tensor.matmul(o, hid[:, a, hc, g * NCMP:(g + 1) * NCMP], w2[:, a, hc, :], start=hc == 0, stop=False)
                        ins = nc.tensor.matmul(o, ones[0:1, 0:NCMP], b2[0:1, a * HD:(a + 1) * HD], start=False, stop=True)
                lane.done(ins, kc_T)
                mix(MIX_LATE)
                pe.wait_ge(kc_ok.handle, 2)
                for g in range(NSA_G):
                    ins = nc.tensor.transpose(ps[:, 6, g * NCMP:(g + 1) * NCMP], kc[:, g * HD:(g + 1) * HD], con[0:NCMP, C_ID:C_ID + NCMP])
                lane.done(ins, kc_T)
                pe.wait_ge(kcT_ok.handle, 1)
                pe.wait_ge(vc_ok.handle, 1)
                pe.wait_ge(mla_nrm.handle, 10)
                pe.wait_ge(gates_ok.handle, 1)
                pe.wait_ge(ev_nrm.handle, 14)
                pe_attention(pe, lane, EVA)
                pe.wait_ge(EVA.o_out.handle, NSA_H + MLA_H)

            def odd_mixer():
                pe.wait_ge(od_nrm.handle, 2)
                for j in range(DSA_KV):
                    for t in range(ST):
                        ins = nc.tensor.transpose(ps[:, 4 + j // 2, (j % 2) * S + t * P:(j % 2) * S + (t + 1) * P],
                                                  od[:, t, O_K + j * HD:O_K + (j + 1) * HD], ident)
                lane.done(ins, dk_T)
                pe.wait_ge(irope.handle, 3)
                for t in range(ST):
                    ins = nc.tensor.transpose(ps[:, 6, t * P:(t + 1) * P], ikd[:, t, :], ident)
                lane.done(ins, dk_T)

                def pair_T(p):
                    if p >= 2:
                        pe.wait_ge(iq_ok.handle, p - 1)
                    for t in range(ST):
                        ins = nc.tensor.transpose(ps[:, p % 2, t * P:(t + 1) * P], od[:, t, O_IQ + p * P:O_IQ + (p + 1) * P], ident)
                    lane.done(ins, iq_T)

                pair_T(0)
                pe.wait_ge(dk_ok.handle, 3)
                for p in range(IDX_H // 2):
                    if p + 1 < IDX_H // 2:
                        pair_T(p + 1)
                    pe.wait_ge(iq_ok.handle, p + 1)
                    for e in range(2):
                        hh = 2 * p + e
                        if hh >= 4:
                            pe.wait_ge(irel.handle, hh - 3)
                        r = slice(e * IDX_D, (e + 1) * IDX_D)
                        nc.tensor.matmul(ps[:, 2 + hh % 4, 0:S], iqT[r, p % 2, P:2 * P], ikT[r, 0:S], start=True, stop=True)
                        ins = nc.tensor.matmul(ps[:, 2 + hh % 4, S:S + P], iqT[r, p % 2, 0:P], ikT[r, 0:P], start=True, stop=True)
                        lane.done(ins, idx_mm)
                pe.wait_ge(irel.handle, IDX_H)
                pe.wait_ge(sel_ok.handle, 1)
                pe.wait_ge(ident_ok.handle, 1)
                pe.wait_ge(od_nrm.handle, 4)
                pe_attention(pe, lane, ODA)
                pe.wait_ge(ODA.o_out.handle, DSA_H)

            for n in range(4):
                if n > 0:
                    pe.wait_ge(gate_ok.handle, 4 * n)
                if n > 0:
                    modulation(n)
                normed(n, range(3))
                if n == 0:
                    modulation(n)
                normed(n, range(3, 8))
                if n == 0:
                    in_proj("ev_in", n, 3, E_COLS, 0)
                    even_mixer()
                    out_side("ev_out", n, 8, h_parts)
                elif n == 2:
                    in_proj("od_in", n, 4, O_COLS, 7)
                    odd_mixer()
                    out_side("od_out", n, 8, h_parts)
                else:
                    up(f"up{n // 2}", n // 2)
                    pe.wait_ge(up_pair.handle, 32 * (n // 2) + 28)
                    out_side(f"down{n // 2}", n, 16, act_parts)

        @block.scalar
        def _(act):
            lane = Lane(act)

            def run(sig_, out_, in_, f, chain=False, **kw):
                if chain:
                    lane.after()
                ins = nc.scalar.activation(out_, in_, f, **kw)
                if sig_ is not None:
                    lane.done(ins, sig_)

            def x_squares(b, scratch=sgate):
                for t in range(ST):
                    run(xsq, scratch[:, 0:2, :].rearrange("p b s -> p (b s)"), x_sb[:, t, b * NB:(b + 1) * NB], ACT.Square, chain=True,
                        scale=D ** -0.5, accum_out=xst[:, b, t:t + 1])

            def x_norm(n):
                act.wait_ge(xsd.handle, 2 * n + 1)
                run(xsq, xst[:, 0, :], xst[:, 0, :], ACT.Sqrt)

            act.wait_ge(prm_ok.handle, 4)
            run(cs_ok, cs[:, :], prm[:, ROWS["c"][0]:ROWS["c"][0] + KT], ACT.Silu)
            act.wait_ge(rev_ok.handle, 1)
            act.dma_start(toeplitz, rev).then_inc(toep_out, 16)
            act.wait_ge(x_in, 16)
            for b in range(4):
                x_squares(b, hT)
            x_norm(0)
            act.wait_ge(toep_out, 16)
            act.dma_start(wide[:, 0:SLOTS * S].rearrange("p (h s) -> p h s", h=SLOTS),
                          bass.AP(toeplitz.tensor, 0, [[1, P], [REV, SLOTS], [1, S]])).then_inc(toep_in, 16)
            act.wait_ge(flipped.handle, 1)
            for b in range(8):
                run(bias_ok, bias[:, 2 * b:2 * b + 2, :], ps[:, b, :].rearrange("p (h s) -> p h s", h=2), ACT.Copy)

            def high(name, u, extra=0, w=UNIT):
                g = PLAN[name] + u
                act.wait_ge(landed[g % RING], extra * 4 + 16 * (g // RING + 1))
                for k in range(UK):
                    part = slice(k * w // UK, (k + 1) * w // UK)
                    run(hi_ok, ring_hi[:, g % RING, part], ring[:, g % RING, part], ACT.Copy)

            def highs(name, u0, u1, extra=0, w=UNIT):
                for u in range(u0, u1):
                    high(name, u, extra, w)

            def normed(n):
                if n > 0:
                    act.wait_ge(res_out.handle, 4 * n)
                    x_squares(3)
                    x_norm(n)
                act.wait_ge(modc_ok.handle, 2 * (n + 1))
                for b in range(8):
                    if b % 2 == 0:
                        act.wait_ge(xT.handle, 8 * n + b + 1)
                        for k in range(2):
                            kt = 2 * b + k
                            run(hT_act, hT[:, kt, :], ps[:, 4 + b % 4, k * S:(k + 1) * S], ACT.Identity,
                                bias=modc[:, 0, kt:kt + 1], scale=modc[:, 1, kt:kt + 1])
                        act.wait_ge(hT_act.handle, hT_act.n)
                    else:
                        act.wait_ge(hT_dve.handle, 8 * n + b + 1)
                    run(h_hi, hT_hi[:, 2 * b:2 * b + 2, :], hT[:, 2 * b:2 * b + 2, :], ACT.Copy)

            def proj(name, pairs, cols, dst, sq):
                def blk(unit_end, bank, c0, n):
                    act.wait_ge(unit_used.handle, unit_end)
                    for t in range(ST):
                        d = dst[:, t, c0:c0 + n] if isinstance(c0, int) else dst[:, t, bass.ds(c0, n)]
                        run(proj_out if t == 1 else None, d, ps[:, bank + t, 0:n], ACT.Copy)

                def squares4(i, at):
                    lane.after()
                    for t in range(ST):
                        for h in range(4):
                            col, c0 = 8 * pairs * t + 4 * at + h, at * NB + h * HD
                            src = dst[:, t, c0:c0 + HD] if isinstance(i, int) else dst[:, t, bass.ds(i * (2 * NB) + c0, HD)]
                            mean = st[:, col:col + 1] if isinstance(i, int) else st[:, bass.ds(i * 8 + col, 1)]
                            run(sq, squared[:, 4 * t + h, :], src, ACT.Square, scale=HD ** -0.5, accum_out=mean)

                highs(name, AHEAD, 8 + AHEAD)
                blk(PLAN[name] + 8, 0, 0, NB)
                squares4(0, 0)
                highs(name, 8 + AHEAD, 16)
                with lane.loop(1, pairs, {hi_ok: 16 * UK, proj_out: 2, sq: 16}, hi_ok) as i:
                    highs(name, 0, AHEAD, i * 16)
                    blk(i * 16 + PLAN[name], 2, i * (2 * NB) - NB, NB)
                    squares4(i, -1)
                    highs(name, AHEAD, 8 + AHEAD, i * 16)
                    blk(i * 16 + (PLAN[name] + 8), 0, i * (2 * NB), NB)
                    squares4(i, 0)
                    highs(name, 8 + AHEAD, 16, i * 16)
                rest = cols - 2 * pairs * NB
                highs(name, 16 * pairs, 16 * pairs + AHEAD, w=UK * rest)
                blk(PLAN[name] + 16 * pairs, 2, (2 * pairs - 1) * NB, NB)
                squares4(0, 2 * pairs - 1)
                highs(name, 16 * pairs + AHEAD, 16 * pairs + 8, w=UK * rest)
                blk(PLAN[name] + 16 * pairs + 8, 0, 2 * pairs * NB, rest)

            def out_side(name, n, units, next_name):
                for u in range(units):
                    if n % 2 == 1:
                        act.wait_ge(up_pair.handle, 32 * (n // 2) + turns_for(u))
                        run(h_hi, act_hi[:, 2 * u:2 * u + 2, :], act_pair(u), ACT.Copy)
                        if u >= AHEAD:
                            high(name, u)
                        if u % 2 == 1 and u < 8:
                            up_tile(n // 2, 28 + u // 2, u // 2, 1)
                    else:
                        run(h_hi, hT_hi[:, 2 * u:2 * u + 2, :], hT[:, 2 * u:2 * u + 2, :], ACT.Copy)
                        if u >= AHEAD:
                            high(name, u)
                highs(name, units, units + AHEAD)
                act.wait_ge(gate_red.handle, n + 1)
                for j in range(4):
                    run(gate_ok, acc[:, 2, j * NB:(j + 1) * NB], ps[:, 4 + j, :], ACT.Copy)
                highs(name, units + AHEAD, units + AHEAD + 5)
                for b in range(3):
                    if n < 3:
                        act.wait_ge(res_out.handle, 4 * n + b + 1)
                        x_squares(b)
                    highs(name, (b + 1) * units + AHEAD + 5, min((b + 2) * units + AHEAD + 5, 4 * units))
                if next_name is not None:
                    highs(next_name, 0, AHEAD)

            def squares(sig_, col, src, width):
                run(sig_, scr[:, 0:width], src, ACT.Square, chain=True, scale=width ** -0.5, accum_out=st[:, col:col + 1])

            def attention(att):
                units, qh = att.units, att.qh

                def queries(n):
                    if n >= len(units) or n not in att.first_of:
                        return
                    q = qh[n]
                    kind, h = units[n]
                    act.wait_ge(att.q_raw.handle, q + 1)
                    if q >= 2:
                        act.wait_ge(att.s_ok.handle, att.last_of[q - 2] + 1)
                    bank = Q_B if kind == "mla" else Q_B + q % 2
                    if kind == "mla":
                        run(None, qpT[:, q % 2, :], ps[0:ROPE, Q_B + 1, 0:S], ACT.Copy, scale=(HD + ROPE) ** -0.5)
                        run(None, knT[:, q % 2, :], ps[:, Q_B, S:2 * S], ACT.Copy, scale=prm[:, ROWS["nope_g"][0] + 1:ROWS["nope_g"][0] + 2])
                    g = {"dsa": 1, "mla": 2}.get(kind, 0)
                    run(att.q_ok, qT[:, q % 2, :], ps[:, bank, 0:S], ACT.Copy, scale=gs[:, g:g + 1])

                def exps(n):
                    kind, h = units[n]
                    act.wait_ge(att.l_ok.handle, n + 1)
                    for t, off, nk in ((1, 0, S), (0, S, P)):
                        if kind == "cmp":
                            off, nk = t * NCMP, NCMP
                        run(att.p_ok if t == 0 else None, L[:, n % 3, off:off + nk], L[:, n % 3, off:off + nk], ACT.Exp, scale=-1.0,
                            bias=nmx[:, n % 3, t:t + 1], accum_out=sm[:, n % 3, t:t + 1])

                def scale(n):
                    kind, h = units[n]
                    act.wait_ge(att.w_ok.handle, n + 1)
                    for t, off, nk in ((1, 0, S), (0, S, P)):
                        if kind == "cmp":
                            off, nk = t * NCMP, NCMP
                        run(att.scaled if t == 0 else None, L[:, n % 3, off:off + nk], L[:, n % 3, off:off + nk], ACT.Copy,
                            scale=rw[:, n % 3, t:t + 1])

                def probs(n):
                    kind, h = units[n]
                    act.wait_ge(att.t_ok.handle, n + 1)
                    if n >= 2:
                        act.wait_ge(att.o_ok.handle, n - 1)
                    if kind == "cmp":
                        run(att.pt_ok, PT[0:NCMP, n % 2, 0:S], ps[0:NCMP, T_B + n % 2, 0:S], ACT.Copy)
                    else:
                        run(att.pt_ok, PT[:, n % 2, :], ps[:, T_B + n % 2, 0:3 * P], ACT.Copy)

                queries(0)
                for n in range(len(units) + LAG):
                    queries(n + 1)
                    if n < len(units):
                        exps(n)
                    if 1 <= n <= len(units):
                        scale(n - 1)
                    if n >= LAG:
                        probs(n - LAG)

            def even_mixer():
                lane.after()
                for t in range(ST):
                    for j, (c0, wd) in enumerate(((E_CQ, Q_RANK), (E_CKV, KV_RANK), (E_KPE, ROPE))):
                        squares(ev_sq, 48 + 3 * t + j, ev[:, t, c0:c0 + wd], wd)
                act.wait_ge(ev_var.handle, 1)
                run(ev_sq, st[:, 0:54], st[:, 0:54], ACT.Sqrt)
                run(gates_raw, ev[:, :, E_GATE:E_GATE + 3 * NSA_H], ev[:, :, E_GATE:E_GATE + 3 * NSA_H], ACT.Sigmoid)
                act.wait_ge(ek_T.handle, 2)
                for b in range(2):
                    run(ek_ok, kT[:, 2 * b:2 * b + 2, :], ps[:, 4 + b, :].rearrange("p (k s) -> p k s", k=2), ACT.Copy,
                        scale=prm[:, ROWS["nsa_g"][0] + 1:ROWS["nsa_g"][0] + 2])
                for b in range(3):
                    act.wait_ge(ek_T.handle, 3 + b)
                    for k in range(2):
                        col = ROWS["qn_g"][0] + 2 * b + k
                        run(ek_ok, hT[:, 8 + 2 * b + k, :], ps[:, 4 + b, k * S:(k + 1) * S], ACT.Copy, scale=prm[:, col:col + 1])
                act.wait_ge(ek_T.handle, 6)
                run(ek_ok, kpT[:, :], ps[0:ROPE, 7, 0:S], ACT.Copy)

                def hidden(a):
                    act.wait_ge(unit_used.handle, mix_end("cmp", a, 7))
                    for hc in range(2):
                        col = ROWS["b1"][0] + 2 * a + hc
                        run(hid_ok, hid[:, a, hc, :], ps[:, 4 + 2 * a + hc, 0:NSA_G * NCMP], ACT.Gelu_apprx_tanh, bias=prm[:, col:col + 1])

                def mla_block(b):
                    act.wait_ge(unit_used.handle, mix_end("mla", b, 1 if b < 3 else 0))
                    for t in range(ST):
                        d = qf[:, t, b * NB:(b + 1) * NB] if b < 3 else kvf[:, t, (b - 3) * NB:(b - 2) * NB]
                        run(mla_out if t == 1 else None, d, ps[:, 2 * (b % 2) + t, :], ACT.Copy)
                    heads = {0: (0, 1), 1: (2, 3, 4), 2: (5, 6, 7)}.get(b, (2 * (b - 3), 2 * (b - 3) + 1))
                    n = 0
                    for t in range(ST):
                        for h in heads:
                            q0, k0 = h * (HD + ROPE), h * 2 * HD
                            for j, src, wd in (((0, qf[:, t, q0:q0 + HD], HD), (1, qf[:, t, q0 + HD:q0 + HD + ROPE], ROPE)) if b < 3
                                               else ((2, kvf[:, t, k0:k0 + HD], HD),)):
                                run(mla_sq, msq[:, n % 6, 0:wd], src, ACT.Square, chain=n % 6 == 0, scale=wd ** -0.5,
                                    accum_out=st[:, 24 * t + 8 * j + h:24 * t + 8 * j + h + 1])
                                n += 1

                act.wait_ge(ev_nrm.handle, 14)
                for kind, a, u in MIX:
                    if (kind, u) == ("cmp", 7):
                        hidden(a)
                    elif kind == "mla" and (a >= 3 or u == 1):
                        mla_block(a)
                        if a == 2:
                            act.wait_ge(mla_var.handle, 1)
                            run(mla_sq, mean_q, mean_q, ACT.Sqrt)
                act.wait_ge(kc_T.handle, 1)
                for g in range(NSA_G):
                    run(kc_sq, scr[0:NCMP, g * HD:(g + 1) * HD], ps[0:NCMP, 4, g * HD:(g + 1) * HD], ACT.Square, scale=HD ** -0.5,
                        accum_out=st[0:NCMP, 60 + g:61 + g])
                act.wait_ge(kc_var.handle, 1)
                run(kc_sq, st[0:NCMP, 60:62], st[0:NCMP, 60:62], ACT.Sqrt)
                for b in (4, 5, 6):
                    mla_block(b)
                act.wait_ge(mla_var.handle, 2)
                run(mla_sq, mean_k, mean_k, ACT.Sqrt)
                act.wait_ge(kc_T.handle, 2)
                run(kcT_ok, kcT, ps[:, 6, 0:NSA_G * NCMP], ACT.Copy, scale=prm[:, ROWS["nsa_g"][0] + 1:ROWS["nsa_g"][0] + 2])
                highs("ev_out", 0, AHEAD)
                attention(EVA)
                act.wait_ge(EVA.o_out.handle, NSA_H + MLA_H)

            def odd_mixer():
                act.wait_ge(od_var.handle, 1)
                run(od_sq, st[:, :], st[:, :], ACT.Sqrt)
                run(ident_ok, ident_r[:, :], ident, ACT.Copy)
                act.wait_ge(dk_T.handle, 1)
                for b in range(2):
                    run(dk_ok, kT[:, 2 * b:2 * b + 2, :], ps[:, 4 + b, :].rearrange("p (k s) -> p k s", k=2), ACT.Copy,
                        scale=prm[:, ROWS["dsa_g"][0] + 1:ROWS["dsa_g"][0] + 2])
                act.wait_ge(dk_T.handle, 2)
                run(dk_ok, ikT, ps[:, 6, 0:S], ACT.Copy)
                for p in range(IDX_H // 2):
                    act.wait_ge(iq_T.handle, p + 1)
                    if p >= 2:
                        act.wait_ge(idx_mm.handle, 2 * p - 2)
                    run(iq_ok, iqT[:, p % 2, :], ps[:, p % 2, 0:S], ACT.Copy)
                    for e in range(2):
                        hh = 2 * p + e
                        act.wait_ge(idx_mm.handle, hh + 1)
                        if hh >= 2:
                            act.wait_ge(isum.handle, hh - 1)
                        run(irel, rel[:, hh % 2, :], ps[:, 2 + hh % 4, 0:3 * P], ACT.Relu)
                highs("od_out", 0, AHEAD)
                attention(ODA)
                act.wait_ge(ODA.o_out.handle, DSA_H)

            def up_tile(f, before, r, s, extra=0):
                q, b = BANK_TURNS[r], r % 2
                if not (isinstance(extra, int) and f == 0 and before < 2):
                    act.wait_ge(up_pair.handle, extra + (32 * f + before - 1))
                for gv in range(2):
                    run(up_conv if gv == 1 else None, cbuf[:, b, gv, :],
                        ps[:, 4 * s + 2 * gv + q // 2, (q % 2) * S:(q % 2 + 1) * S], ACT.Identity,
                        bias=cw_now[:, s, 3, gv, q:q + 1], scale=cw_now[:, s, 2, gv, q:q + 1])
                act.wait_ge(gconv.handle, extra + (32 * f + before + 1))
                run(up_silu, sgate[:, b, :], cbuf[:, b, 0, :], ACT.Silu)

            def up(name, f):
                def one_pass(i):
                    for s in range(2):
                        first = isinstance(i, int) and s == 0
                        for u in range(16):
                            if not (first and u < AHEAD):
                                high(name, 16 * s + u, i * 32)
                            if not first and u % 4 == 2:
                                if u == 2:
                                    act.wait_ge(cw_ok.handle, i * 4 + (16 * f + 2 * s))
                                    act.wait_ge(unit_used.handle, i * 32 + (PLAN[name] + 16 * s))
                                up_tile(f, 4 * s - 4 + u // 4, u // 4, 1 - s, i * 8)
                one_pass(0)
                with lane.loop(1, 4, {hi_ok: 32 * UK, up_conv: 8, up_silu: 8}, hi_ok) as i:
                    one_pass(i)
                highs(f"down{f}", 0, AHEAD)
                act.wait_ge(cw_ok.handle, 16 * (f + 1))
                act.wait_ge(unit_used.handle, PLAN[name] + 128)

            highs("ev_in", 0, AHEAD)
            for n in range(4):
                normed(n)
                if n == 0:
                    proj("ev_in", 3, E_COLS, ev, ev_sq)
                    even_mixer()
                    out_side("ev_out", n, 8, "up0")
                elif n == 2:
                    proj("od_in", 4, O_COLS, od, od_sq)
                    odd_mixer()
                    out_side("od_out", n, 8, "up1")
                else:
                    up(f"up{n // 2}", n // 2)
                    out_side(f"down{n // 2}", n, 16, "od_in" if n == 1 else None)

        @block.vector
        def _(dve):
            lane = Lane(dve)
            v = nc.vector

            def put(ins, sig_=None):
                lane.done(ins, sig_ if sig_ is not None else dve_s)

            dve.wait_ge(prm_T.handle, 1)
            for a, b in ((0, ROWS_A), (PE_COL, PE_COL + 2 * CMP_BLOCK), (CW_COL, 4 * P), (4 * P, PRM)):
                put(v.tensor_copy(prm[:, a:b], ps[:, a // 512, a % 512:a % 512 + b - a]), prm_ok)
            dve.wait_ge(rev_mm.handle, 1)
            put(v.tensor_tensor(rev, ps[0:SLOTS, 2, 0:REV], negrow, ALU.add), rev_ok)
            lane.after()
            for j, (name, sc) in enumerate((("nsa_g", HD ** -0.5), ("dsa_g", HD ** -0.5), ("nope_g", (HD + ROPE) ** -0.5))):
                put(v.tensor_scalar(gs[:, j:j + 1], prm[:, ROWS[name][0]:ROWS[name][0] + 1], sc, None, ALU.mult))
            dve.wait_ge(cs_ok.handle, 1)

            def mod_unit(m, t, col, extra=0):
                slot, landed_, before = mod_slot(m)
                dve.wait_ge(landed_, extra * (4 if m < FIRST_MOD else 8) + 16 * (before + 1))
                lane.after()
                put(v.scalar_tensor_tensor(acc[:, t, :], slot, col, acc[:, t, :], ALU.mult, ALU.add), ada_used)

            def sums_cleared(n):
                dve.wait_ge(acc_clear.handle, CLEARED[n + 1])
                dve.wait_ge(acc_bias, 16 * CLEARED[n + 1])

            def first_sums():
                sums_cleared(-1)

                def one_pass(i):
                    lane.after()
                    put(v.tensor_copy(cs_now[:, 0:2], cs[:, 0:2] if isinstance(i, int) else cs[:, bass.ds(i * 2, 2)]))
                    for j in range(4):
                        mod_unit(j, j % 2, cs_now[:, j // 2:j // 2 + 1], i * 4)
                one_pass(0)
                dve.wait_ge(cb_mm.handle, 1)
                put(v.tensor_tensor(cbias[:, :, :, :].rearrange("p t j h -> p (t j) h"),
                                    ps[:, 3, 0:ST * NCMP * NSA_H].rearrange("p (a h) -> p a h", h=NSA_H),
                                    con[:, C_CMASK:C_VALID].unsqueeze(2).broadcast_to([P, ST * NCMP, NSA_H]), ALU.add), cb_ok)
                normed(0)
                with lane.loop(1, KT // 2, {ada_used: 4, dve_s: 1}, ada_used) as i:
                    one_pass(i)

            def loop_cs(n, i):
                k = len(MOD_PASS[n]) // 2 - 2
                lane.after()
                for at, c_ in ((0, 4), (4, k)):
                    if c_ > 0:
                        put(v.tensor_copy(cs_now[:, at:at + c_], cs[:, 0:c_] if isinstance(i, int) else cs[:, bass.ds(i * c_, c_)]))

            def loop_unit(n, j, i):
                t, _, k = MOD_PASS[n][j]
                at = k if t == 2 else 4 + k
                mod_unit(first_mod(n) + j, t, cs_now[:, at:at + 1], i * len(MOD_PASS[n]))

            CMP_REST, INDEX_REST = 3, 8
            rest_at = [0] * 4

            def rest_unit(n):
                j = rest_at[n]
                if j < len(MOD_REST[n]):
                    t, k = MOD_REST[n][j]
                    mod_unit(first_mod(n) + len(MOD_PASS[n]) * MOD_PASSES[n] + j, t, cs[:, k:k + 1])
                    rest_at[n] += 1

            def normed(n):
                dve.wait_ge(xsq.handle, 9 * n + 8)
                put(v.tensor_tensor(xst[:, 0:2, :], xst[:, 0:2, :], xst[:, 2:4, :], ALU.add))
                lane.after()
                put(v.scalar_tensor_tensor(xst[:, 0, :], xst[:, 0, :], EPS, xst[:, 1, :], ALU.add, ALU.add), xsd)
                dve.wait_ge(xsq.handle, 9 * n + 9)
                put(v.reciprocal(xst[:, 0, :], xst[:, 0, :]), xsd)
                lane.after()
                put(v.tensor_scalar(xn[:, 0, :], x_sb[:, 0, :], xst[:, 0, 0:1], None, ALU.mult), xn_ok)
                put(v.tensor_scalar(xn[:, 1, :], x_sb[:, 1, :], xst[:, 0, 1:2], None, ALU.mult), xn_ok)

            def low(name, u, extra=0, w=UNIT):
                g = (PLAN[name] + u) % RING
                for k in range(UK):
                    part = slice(k * w // UK, (k + 1) * w // UK)
                    dve.wait_ge(hi_ok.handle, extra * UK + nth(name, u, k))
                    put(v.tensor_tensor(ring_lo[:, g, part], ring[:, g, part], ring_hi[:, g, part].bitcast(F32), ALU.subtract), lo_ok)

            def lows(name, u0, u1, extra=0, w=UNIT):
                for u in range(u0, u1):
                    low(name, u, extra, w)

            def low_pair(nth_pair, lo, value, hi):
                dve.wait_ge(h_hi.handle, nth_pair + 1)
                put(v.tensor_tensor(lo, value, hi.bitcast(F32), ALU.subtract), h_lo)

            def low_hT(before, b):
                k = slice(2 * b, 2 * b + 2)
                low_pair(before + b, hT_lo[:, k, :], hT[:, k, :], hT_hi[:, k, :])

            def modulate(n):
                dve.wait_ge(cols_done.handle, n + 1)
                put(v.tensor_copy(modc[:, 0, :], ps[:, 7, 0:KT]), modc_ok)
                g0 = ROWS["norm_g"][0] + n * KT
                put(v.scalar_tensor_tensor(modc[:, 1, :], ps[:, 7, KT:2 * KT], 1.0, prm[:, g0:g0 + KT], ALU.add, ALU.mult), modc_ok)
                lane.after()
                before = PAIRS_BEFORE[n, "in"]
                for b in range(1, 8, 2):
                    dve.wait_ge(xT.handle, 8 * n + b + 1)
                    for k in range(2):
                        kt = 2 * b + k
                        put(v.tensor_scalar(hT[:, kt, :], ps[:, 4 + b % 4, k * S:(k + 1) * S], modc[:, 1, kt:kt + 1],
                                            modc[:, 0, kt:kt + 1], ALU.mult, ALU.add), hT_dve)
                    if b > 1:
                        low_hT(before, b - 2)
                    low_hT(before, b - 1)
                low_hT(before, 7)

            def due(u, units, per):
                return (u + 1) * per // units > u * per // units

            def residual(name, n, units, b):
                if b == 0:
                    dve.wait_ge(gate_ok.handle, 4 * (n + 1))
                dve.wait_ge(unit_used.handle, PLAN[name] + units * (b + 1))
                cols = slice(b * NB, (b + 1) * NB)
                lane.after()
                for t in range(ST):
                    put(v.tensor_tensor(rtmp[:, t, :], ps[:, 2 * (b % 2) + t, :], acc[:, 2, cols], ALU.mult))
                lane.after()
                for t in range(ST):
                    put(v.tensor_tensor(x_sb[:, t, cols], x_sb[:, t, cols], rtmp[:, t, :], ALU.add), res_out if t == 1 else None)

            def out_side(name, n, units, next_name):
                before = PAIRS_BEFORE[n, "out"]
                for u in range(units):
                    if n % 2 == 1:
                        low_pair(before + u, act_lo[:, 2 * u:2 * u + 2, :], act_pair(u), act_hi[:, 2 * u:2 * u + 2, :])
                    else:
                        low_hT(before, u)
                    if u >= AHEAD:
                        low(name, u)
                    if n % 2 == 1 and u % 2 == 1 and u < 8:
                        q = BANK_TURNS[u // 2]
                        up_tile(n // 2, 28 + u // 2, u // 2, 1, actF[:, (28 + q) * S:(29 + q) * S])
                late = len(MOD_REST[n]) - rest_at[n]

                def more(u0, u1):
                    for u in range(u0, u1):
                        low(name, u)
                        if due(u - units, 5 * units // 2, late):
                            rest_unit(n)
                more(units, units + AHEAD + 2)
                residual(name, n, units, 0)
                more(units + AHEAD + 2, 2 * units + AHEAD)
                residual(name, n, units, 1)
                more(2 * units + AHEAD, 3 * units + AHEAD)
                residual(name, n, units, 2)
                more(3 * units + AHEAD, 4 * units)
                if next_name is not None:
                    lows(next_name, 0, AHEAD)
                residual(name, n, units, 3)

            def in_proj(name, n, pairs, cols):
                per = len(MOD_PASS[n])
                sums_cleared(n)

                def one_pass(i):
                    loop_cs(n, i)
                    j = 0
                    for u in range(16):
                        if not (isinstance(i, int) and u < AHEAD):
                            low(name, u, i * 16)
                        if due(u, 16, per):
                            loop_unit(n, j, i)
                            j += 1
                one_pass(0)
                with lane.loop(1, pairs, {dve_s: 2, lo_ok: 16 * UK, ada_used: per}, ada_used) as i:
                    one_pass(i)
                for u in range(8):
                    low(name, 16 * pairs + u, w=UK * (cols - 2 * pairs * NB))
                    if u % 2 == 1 and rest_at[n] < GATE_UNITS[n] - per * pairs:
                        rest_unit(n)

            def rotate(x1, x2, cos, sin, tmp, sig_):
                a, b, c_, d_ = tmp
                lane.after()
                put(v.tensor_tensor(a, x1, cos, ALU.mult))
                put(v.tensor_tensor(b, x2, sin, ALU.mult))
                put(v.tensor_tensor(c_, x1, sin, ALU.mult))
                put(v.tensor_tensor(d_, x2, cos, ALU.mult))
                lane.after()
                put(v.tensor_tensor(x1, a, b, ALU.subtract))
                put(v.tensor_tensor(x2, c_, d_, ALU.add), sig_)

            def scale_heads(x3, r, heads, sig_):
                put(v.tensor_tensor(x3, x3, r.unsqueeze(2).broadcast_to([P, heads, x3.shape[2]]), ALU.mult), sig_)

            def attention(att, n_sub, every):
                units, qh = att.units, att.qh

                def logits(n):
                    kind, h = units[n]
                    dve.wait_ge(att.s_ok.handle, n + 1)
                    if n >= 3:
                        dve.wait_ge(att.t_ok.handle, n - 2)
                    lane.after()
                    src = ps[:, S_B + n % 2, :]
                    l = L[:, n % 3, :]
                    for t, off, nk in ((1, 0, S), (0, S, P)):
                        if kind == "cmp":
                            i0, o, b = src[:, t * P:t * P + NCMP], l[:, t * NCMP:(t + 1) * NCMP], cbias[:, t, :, h]
                        else:
                            i0, o = src[:, off:off + nk], l[:, off:off + nk]
                            b0 = 0 if t == 1 else P
                            b = causal[:, b0:S] if kind == "mla" else bias[:, h, b0:S]
                        put(v.tensor_tensor_reduce(o, i0, b, -1.0, -TAKEN, ALU.add, ALU.min, nmx[:, n % 3, t:t + 1]),
                            att.l_ok if t == 0 else None)

                def weights(n):
                    kind, h = units[n]
                    dve.wait_ge(att.p_ok.handle, n + 1)
                    lane.after()
                    gated = kind in ("cmp", "slc", "win")
                    put(v.reciprocal(rw[:, n % 3, :], sm[:, n % 3, :]), None if gated else att.w_ok)
                    if gated:
                        lane.after()
                        col = E_GATE + 3 * h + ("cmp", "slc", "win").index(kind)
                        put(v.tensor_tensor(rw[:, n % 3, :], rw[:, n % 3, :], ev[:, :, col], ALU.mult), att.w_ok)

                def output(n):
                    if n not in att.last_of:
                        return
                    q = qh[n]
                    dve.wait_ge(att.o_ok.handle, n + 1)
                    put(v.tensor_copy(hT[:, q, :], ps[:, O_B + q % 2, 0:S]), att.o_out)

                for n in range(len(units) + 5):
                    if n < len(units):
                        logits(n)
                    if 0 <= n - 1 < len(units):
                        weights(n - 1)
                    if 0 <= n - 4 < len(units):
                        output(n - 4)
                    if n % every == every - 1:
                        rest_unit(n_sub)

            def even_mixer():
                dve.wait_ge(ek_T.handle, 1)
                for a in range(2):
                    for g in range(NSA_G):
                        for hh in range(2):
                            src = ps[:, 6 + a, g * S + 16 * hh:g * S + 16 * hh + 240].rearrange("p (j l) -> p j l", l=16)
                            dst = flat[:, a, 16 * hh:16 * hh + 16, g * NCMP:(g + 1) * NCMP].rearrange("p l j -> p j l")
                            pe_ = prm[:, PE_COL + a * 32 + 16 * hh:PE_COL + a * 32 + 16 * hh + 16]
                            put(v.tensor_tensor(dst, src, pe_.unsqueeze(1).broadcast_to([P, NCMP, 16]), ALU.add), flat_ok)
                dve.wait_ge(ev_sq.handle, 54)
                put(v.tensor_scalar(st[:, 0:54], st[:, 0:54], EPS, None, ALU.add), ev_var)
                dve.wait_ge(ev_sq.handle, 55)
                put(v.reciprocal(st[:, 0:54], st[:, 0:54]))
                lane.after()
                for t in range(ST):
                    r = st[:, 24 * t:24 * t + 24]
                    hd = lambda c0, k: ev[:, t, c0:c0 + k * HD].rearrange("p (h d) -> p h d", h=k)
                    scale_heads(hd(kv_col(2, 0), 2), r[:, 12:14], 2, ev_nrm)
                    scale_heads(hd(kv_col(4, 0), 2), r[:, 16:18], 2, ev_nrm)
                    for j, (c0, wd) in enumerate(((E_CQ, Q_RANK), (E_CKV, KV_RANK))):
                        put(v.tensor_scalar(ev[:, t, c0:c0 + wd], ev[:, t, c0:c0 + wd], st[:, 48 + 3 * t + j:49 + 3 * t + j],
                                            None, ALU.mult), ev_nrm)
                    put(v.scalar_tensor_tensor(ev[:, t, E_KPE:E_KPE + ROPE], ev[:, t, E_KPE:E_KPE + ROPE], st[:, 50 + 3 * t:51 + 3 * t],
                                               ropeg[:, ROPE:2 * ROPE], ALU.mult, ALU.mult), ev_nrm)
                H2 = ROPE // 2
                for t in range(ST):
                    cos, sin = (con[:, c0 + t * H2:c0 + (t + 1) * H2] for c0 in (C_COS64, C_SIN64))
                    rotate(ev[:, t, E_KPE:E_KPE + H2], ev[:, t, E_KPE + H2:E_KPE + ROPE], cos, sin,
                           [scr[:, j * H2:(j + 1) * H2] for j in range(4)], ev_nrm)
                for t in range(ST):
                    scale_heads(ev[:, t, E_Q:E_Q + NSA_H * HD].rearrange("p (h d) -> p h d", h=NSA_H), st[:, 24 * t:24 * t + 8], NSA_H, ev_nrm)
                dve.wait_ge(gates_raw.handle, 1)
                gc = ev[:, :, E_GATE:E_GATE + 3 * NSA_H].rearrange("p t (h c) -> p t h c", c=3)[:, :, :, 0]
                put(v.tensor_tensor(gc, gc, valid.unsqueeze(2).broadcast_to([P, ST, NSA_H]), ALU.mult), gates_ok)
                for _ in range(CMP_REST):
                    rest_unit(0)
                dve.wait_ge(mla_sq.handle, 32)
                put(v.tensor_scalar(mean_q, mean_q, EPS, None, ALU.add), mla_var)
                dve.wait_ge(mla_sq.handle, 32 + 1)
                put(v.reciprocal(mean_q, mean_q))
                lane.after()
                for t in range(ST):
                    q3 = qf[:, t, :].rearrange("p (h d) -> p h d", h=MLA_H)
                    scale_heads(q3[:, :, 0:HD], mean_q[:, t, 0:8], MLA_H, mla_nrm)
                    scale_heads(q3[:, :, HD:HD + ROPE], mean_q[:, t, 8:16], MLA_H, mla_nrm)
                    lane.after()
                    put(v.tensor_tensor(q3[:, :, HD:HD + ROPE], q3[:, :, HD:HD + ROPE],
                                        ropeg[:, 0:ROPE].unsqueeze(1).broadcast_to([P, MLA_H, ROPE]), ALU.mult), mla_nrm)
                    cos, sin = (con[:, c0 + t * H2:c0 + (t + 1) * H2].unsqueeze(1).broadcast_to([P, MLA_H, H2])
                                for c0 in (C_COS64, C_SIN64))
                    tmp = [L[:, :, :].rearrange("p b s -> p (b s)")[:, j * 256:(j + 1) * 256].rearrange("p (h d) -> p h d", h=MLA_H)
                           for j in range(4)]
                    rotate(q3[:, :, HD:HD + H2], q3[:, :, HD + H2:HD + ROPE], cos, sin, tmp, mla_nrm)
                dve.wait_ge(kc_sq.handle, 2)
                put(v.tensor_scalar(st[0:NCMP, 60:62], st[0:NCMP, 60:62], EPS, None, ALU.add), kc_var)
                put(v.tensor_copy(vc[:, :], ps[0:NCMP, 5, 0:NSA_G * HD]), vc_ok)
                dve.wait_ge(kc_sq.handle, 3)
                put(v.reciprocal(st[0:NCMP, 60:62], st[0:NCMP, 60:62]))
                lane.after()
                for g in range(NSA_G):
                    put(v.tensor_scalar(kc[:, g * HD:(g + 1) * HD], ps[0:NCMP, 4, g * HD:(g + 1) * HD], st[0:NCMP, 60 + g:61 + g],
                                        None, ALU.mult), kc_ok)
                dve.wait_ge(mla_sq.handle, 32 + 16 + 1)
                put(v.tensor_scalar(mean_k, mean_k, EPS, None, ALU.add), mla_var)
                dve.wait_ge(mla_sq.handle, 32 + 16 + 2)
                put(v.reciprocal(mean_k, mean_k))
                lane.after()
                for t in range(ST):
                    scale_heads(kvf[:, t, :].rearrange("p (h d) -> p h d", h=MLA_H)[:, :, 0:HD], mean_k[:, t, :], MLA_H, mla_nrm)
                lows("ev_out", 0, AHEAD)
                dve.wait_ge(bias_ok.handle, 8)
                attention(EVA, 0, 2)

            def odd_mixer():
                Hf = IDX_ROPE // 2
                dve.wait_ge(proj_out.handle, 16)
                for t in range(ST):
                    iq3 = od[:, t, O_IQ:O_IK].rearrange("p (h d) -> p h d", h=IDX_H)
                    c1, s1 = (con[:, c0 + t * Hf:c0 + (t + 1) * Hf] for c0 in (C_COS32, C_SIN32))
                    c3, s3 = (a.unsqueeze(1).broadcast_to([P, IDX_H, Hf]) for a in (c1, s1))
                    tmp = [scr[:, 2048 + j * 256:2048 + (j + 1) * 256].rearrange("p (h d) -> p h d", h=IDX_H) for j in range(4)]
                    rotate(iq3[:, :, 0:Hf], iq3[:, :, Hf:2 * Hf], c3, s3, tmp, None)
                    ik = od[:, t, O_IK:O_IW]
                    rotate(ik[:, 0:Hf], ik[:, Hf:2 * Hf], c1, s1, [scr[:, 3072 + j * Hf:3072 + (j + 1) * Hf] for j in range(4)], None)
                lane.after()
                put(v.tensor_scalar(od[:, :, O_IW:O_COLS], od[:, :, O_IW:O_COLS], IDX_H ** -0.5 * IDX_D ** -0.5, None, ALU.mult), irope)
                for e in range(2):
                    put(v.tensor_copy(ikd[:, :, e * IDX_D:(e + 1) * IDX_D], od[:, :, O_IK:O_IW]), irope)
                dve.wait_ge(od_sq.handle, 64)
                put(v.tensor_scalar(st[:, :], st[:, :], EPS, None, ALU.add), od_var)
                dve.wait_ge(od_sq.handle, 65)
                put(v.reciprocal(st[:, :], st[:, :]))
                lane.after()
                for t in range(ST):
                    scale_heads(od[:, t, O_K:O_V].rearrange("p (h d) -> p h d", h=DSA_KV), st[:, 32 * t + 16:32 * t + 20], DSA_KV, od_nrm)
                for t in range(ST):
                    scale_heads(od[:, t, 0:O_K].rearrange("p (h d) -> p h d", h=DSA_H), st[:, 32 * t:32 * t + 16], DSA_H, od_nrm)
                for hh in range(IDX_H):
                    dve.wait_ge(irel.handle, hh + 1)
                    lane.after()
                    for t, off, nk in ((1, 0, S), (0, S, P)):
                        w = od[:, t, O_IW + hh:O_IW + hh + 1]
                        r = rel[:, hh % 2, off:off + nk]
                        o = isc[:, off:off + nk]
                        if hh == 0:
                            ins = v.tensor_scalar(o, r, w, None, ALU.mult)
                        else:
                            ins = v.scalar_tensor_tensor(o, r, w, o, ALU.mult, ALU.add)
                        put(ins, isum if t == 0 else None)
                    if due(hh, IDX_H, INDEX_REST):
                        rest_unit(2)
                lane.after()
                for t, off, nk in ((1, 0, S), (0, S, P)):
                    o = isc[:, off:off + nk]
                    put(v.tensor_tensor(o, o, causal[:, S - nk:S], ALU.add))
                lane.after()
                for r in range(TOPK // 8):
                    for step in range(2):
                        for t, off, nk in ((1, 0, S), (0, S, P)):
                            cur, work = (isc if r == 0 else iwk)[:, off:off + nk], iwk[:, off:off + nk]
                            if (r, step) != (0, 0):
                                dve.wait_ge(dve_s.handle, dve_s.n - 1)
                            if step == 0:
                                put(v.max(m8[:, t, :], cur))
                            else:
                                put(v.match_replace(work, m8[:, t, :], cur, TAKEN))
                lane.after()
                put(v.tensor_scalar(selm[:, :], iwk, TAKEN / 2, NEG, ALU.is_gt, ALU.mult), sel_ok)
                lows("od_out", 0, AHEAD)
                attention(ODA, 2, 2)

            def up_tile(f, before, r, s, dst, extra=0):
                q, b = BANK_TURNS[r], r % 2
                dve.wait_ge(up_conv.handle, extra + (32 * f + before + 1))
                for gv in range(2):
                    for tap in range(2):
                        d = tap + 1
                        u = ps[:, 4 * s + 2 * gv + q // 2, (q % 2) * S:(q % 2 + 1) * S - d]
                        cb = cbuf[:, b, gv, d:S]
                        lane.after()
                        put(v.scalar_tensor_tensor(cb, u, cw_now[:, s, 1 - tap, gv, q:q + 1], cb, ALU.mult, ALU.add),
                            gconv if (gv == 0 and tap == 1) else None)
                dve.wait_ge(up_silu.handle, extra + (32 * f + before + 1))
                lane.after()
                put(v.tensor_tensor(dst, sgate[:, b, :], cbuf[:, b, 1, :], ALU.mult), up_pair)

            def up(name, f):
                n = 2 * f + 1
                per = len(MOD_PASS[n])
                cw4 = prm[:, CW_COL + f * 6 * FT:CW_COL + (f + 1) * 6 * FT].rearrange("p (j g t) -> p j g t", j=3, g=2)
                cb3 = prm[:, CB_COL + f * 2 * FT:CB_COL + (f + 1) * 2 * FT].rearrange("p (g t) -> p g t", g=2)
                sums_cleared(n)

                def four(i, step, at):
                    return slice(at, at + 4) if isinstance(i, int) else bass.ds(i * step + at, 4)

                def one_pass(i):
                    loop_cs(n, i)
                    j = 0
                    for s in range(2):
                        first = isinstance(i, int) and s == 0
                        put(v.tensor_copy(cw_now[:, s, 0:3, :, :], cw4[:, :, :, four(i, 8, 4 * s)]), cw_ok)
                        put(v.tensor_copy(cw_now[:, s, 3, :, :], cb3[:, :, four(i, 8, 4 * s)]), cw_ok)
                        for u in range(16):
                            if not (first and u < AHEAD):
                                low(name, 16 * s + u, i * 32)
                            if not first and u % 4 == 2:
                                at = 4 * s - 4 + BANK_TURNS[u // 4]
                                dst = actF[:, at * S:(at + 1) * S] if isinstance(i, int) else actF[:, bass.ds(i * (8 * S) + at * S, S)]
                                up_tile(f, 4 * s - 4 + u // 4, u // 4, 1 - s, dst, i * 8)
                            if u % 4 == 0 and due(u // 4, 4, per // 2):
                                loop_unit(n, j, i)
                                j += 1
                one_pass(0)
                with lane.loop(1, 4, {dve_s: (2 if n < 3 else 1) + 8 * 3, cw_ok: 4, gconv: 8, up_pair: 8, lo_ok: 32 * UK, ada_used: per}, lo_ok) as i:
                    one_pass(i)
                lows(f"down{f}", 0, AHEAD)

            first_sums()
            lows("ev_in", 0, AHEAD)
            for n in range(4):
                if n > 0:
                    normed(n)
                modulate(n)
                if n == 0:
                    in_proj("ev_in", n, 3, E_COLS)
                    even_mixer()
                    out_side("ev_out", n, 8, "up0")
                elif n == 2:
                    in_proj("od_in", n, 4, O_COLS)
                    odd_mixer()
                    out_side("od_out", n, 8, "up1")
                else:
                    up(f"up{n // 2}", n // 2)
                    out_side(f"down{n // 2}", n, 16, "od_in" if n == 1 else None)


INPUTS = ["x", "c", "rel_bias", "ada_w", "ada_b", "norm_g", "ev_w_in", "ev_w_out", "nsa_qk_g", "cmp_pe", "cmp_w1", "cmp_b1",
          "cmp_w2", "cmp_b2", "mla_q_norm_g", "mla_kv_norm_g", "mla_w_uq", "mla_w_ukv", "mla_nope_g", "mla_rope_g",
          "od_w_in", "od_w_out", "dsa_qk_g", "ffn_w_up", "ffn_conv_w", "ffn_conv_b", "ffn_w_down"]


def kernel(**inputs):
    import concourse.bacc as bacc
    from concourse.bass_utils import run_bass_kernel_spmd

    nc = bacc.Bacc("TRN2", target_bir_lowering=False, num_devices=1)
    arrays = {n: np.ascontiguousarray(inputs[n]) for n in INPUTS} | constants()
    aps = {n: nc.dram_tensor(f"in_{n}", a.shape, mybir.dt.from_np(a.dtype), kind="ExternalInput").ap() for n, a in arrays.items()}
    out = nc.dram_tensor("out", (1, S, D), F32, kind="ExternalOutput").ap()
    trunk_program(nc, **aps, out=out)
    r = run_bass_kernel_spmd(nc, [{f"in_{n}": a for n, a in arrays.items()}], core_ids=[0])
    return r.results[0]["out"]
```
